# Optimizing a Trainium2 kernel written in Bass

```python
import jax, jax.numpy as jnp
from jax import lax
import numpy as np

D_MODEL = 1024
BATCH = 1
SEQ = 512
DEPTH = 2

GRID_W = 64
CTX_LEN = 256
N_MIXERS = 2
RET_HEADS = 4
RET_QK_DIM = D_MODEL // RET_HEADS
RET_V_DIM = 2 * D_MODEL // RET_HEADS
RET_CHUNK = 128
ROPE_BASE = 10000.0
NA_HEADS = 16
NA_HEAD_DIM = D_MODEL // NA_HEADS
NA_MAX_KH = 8
NA_KW = 16
FFN_DIM = 2816
CONV_W = 3
NORM_EPS = 1e-6

kernel_name = "hybrid_retention_natten_convffn_dit"

def _rmsnorm(x, w):
    xf = x.astype(jnp.float32)
    y = xf * lax.rsqrt(jnp.mean(xf * xf, axis=-1, keepdims=True) + NORM_EPS)
    return (y * w.astype(jnp.float32)).astype(x.dtype)

def _modulate(h, shift, scale):
    return h * (1 + scale) + shift

def _axial_rope(x, pos_r, pos_c):
    half = x.shape[-1] // 2
    quarter = half // 2
    inv = ROPE_BASE ** (-jnp.arange(quarter, dtype=jnp.float32) / quarter)

    def rot(xp, pos):
        ang = pos[:, None] * inv[None, :]
        cos = jnp.cos(ang)[None, :, None, :]
        sin = jnp.sin(ang)[None, :, None, :]
        x1, x2 = xp[..., :quarter], xp[..., quarter:]
        return jnp.concatenate([x1 * cos - x2 * sin, x2 * cos + x1 * sin], axis=-1)

    return jnp.concatenate([rot(x[..., :half], pos_r), rot(x[..., half:], pos_c)], axis=-1)

def _retention_scan(q, k, v, log_g, s0, strict):
    b, l, h, _ = q.shape
    dv = v.shape[-1]
    n = l // RET_CHUNK

    def blocks(a):
        return a.reshape(b, n, RET_CHUNK, h, a.shape[-1]).transpose(1, 0, 3, 2, 4)

    idx = jnp.arange(RET_CHUNK, dtype=jnp.float32)
    diff = idx[:, None] - idx[None, :]
    mask = diff > 0 if strict else diff >= 0
    dmat = jnp.where(mask, jnp.exp(log_g[:, None, None] * jnp.maximum(diff, 0.0)), 0.0)
    q_dec = jnp.exp(log_g[:, None] * (idx + 1.0))[..., None]
    k_dec = jnp.exp(log_g[:, None] * (RET_CHUNK - 1.0 - idx))[..., None]
    c_dec = jnp.exp(log_g * RET_CHUNK)[:, None, None]

    def step(state, blk):
        qb, kb, vb = blk
        inner = jnp.einsum('bhij,bhjv->bhiv', jnp.einsum('bhid,bhjd->bhij', qb, kb) * dmat, vb)
        cross = jnp.einsum('bhid,bhdv->bhiv', qb * q_dec, state)
        state = state * c_dec + jnp.einsum('bhjd,bhjv->bhdv', kb * k_dec, vb)
        return state, inner + cross

    s_final, out = lax.scan(step, s0, (blocks(q), blocks(k), blocks(v)))
    return out.transpose(1, 0, 3, 2, 4).reshape(b, l, h, dv), s_final

def _retention(h, hc, w_in, dlog_f, dlog_b, w_out, pos_r, pos_c):
    hk = RET_HEADS * RET_QK_DIM
    hv = RET_HEADS * RET_V_DIM

    def proj(z):
        b, l, _ = z.shape
        q, k, v, g = jnp.split(z @ w_in, [hk, 2 * hk, 2 * hk + hv], axis=-1)
        hd = lambda a, d: a.reshape(b, l, RET_HEADS, d).astype(jnp.float32)
        return hd(q, RET_QK_DIM), hd(k, RET_QK_DIM) * RET_QK_DIM ** -0.5, hd(v, RET_V_DIM), hd(g, RET_V_DIM)

    ql, kl, vl, gl = proj(h)
    qc, kc, vc, gc = proj(hc)
    ql = _axial_rope(ql, pos_r, pos_c)
    kl = _axial_rope(kl, pos_r, pos_c)
    log_gf = -jnp.exp(dlog_f.astype(jnp.float32))
    log_gb = -jnp.exp(dlog_b.astype(jnp.float32))
    zero = jnp.zeros((h.shape[0], RET_HEADS, RET_QK_DIM, RET_V_DIM), jnp.float32)
    flip = lambda a: jnp.flip(a, axis=1)
    oc_f, sc_f = _retention_scan(qc, kc, vc, log_gf, zero, False)
    ol_f, _ = _retention_scan(ql, kl, vl, log_gf, sc_f, False)
    oc_b, sc_b = _retention_scan(flip(qc), flip(kc), flip(vc), log_gb, zero, True)
    ol_b, _ = _retention_scan(flip(ql), flip(kl), flip(vl), log_gb, sc_b, True)

    def out(o, g, dtype):
        b, l = o.shape[:2]
        o = o * lax.rsqrt(jnp.mean(o * o, axis=-1, keepdims=True) + NORM_EPS)
        return (jax.nn.silu(g) * o).reshape(b, l, hv).astype(dtype) @ w_out

    return out(ol_f + flip(ol_b), gl, h.dtype), out(oc_f + flip(oc_b), gc, hc.dtype)

def _neighbourhood_attention(h, hc, w_qkv, rpb, w_out, rows, with_ctx_out):
    b, s, d = h.shape
    kh = min(NA_MAX_KH, rows)
    kw = NA_KW
    scale = NA_HEAD_DIM ** -0.5

    def proj(z):
        q, k, v = jnp.split(z @ w_qkv, 3, axis=-1)
        hd = lambda a: a.reshape(z.shape[0], z.shape[1], NA_HEADS, NA_HEAD_DIM)
        return hd(q) * scale, hd(k), hd(v)

    ql, kl, vl = proj(h)
    qc, kc, vc = proj(hc)
    grid = lambda a: a.reshape(b, rows, GRID_W, NA_HEADS, NA_HEAD_DIM)
    qg, kg, vg = grid(ql), grid(kl), grid(vl)
    cols = jnp.arange(GRID_W)
    cs = jnp.clip(cols - kw // 2, 0, GRID_W - kw)
    col_valid = (cols[None, :] >= cs[:, None]) & (cols[None, :] < cs[:, None] + kw)
    dc_idx = jnp.clip(cols[None, :] - cols[:, None] + kw - 1, 0, 2 * kw - 2)
    rpb_c = rpb[:, :, dc_idx]
    n_loc = kh * GRID_W

    def row_block(r):
        rs = jnp.clip(r - kh // 2, 0, rows - kh)
        q_r = lax.dynamic_index_in_dim(qg, r, axis=1, keepdims=False)
        k_b = lax.dynamic_slice_in_dim(kg, rs, kh, axis=1)
        v_b = lax.dynamic_slice_in_dim(vg, rs, kh, axis=1)
        dr_idx = rs + jnp.arange(kh) - r + kh - 1
        bias = jnp.take(rpb_c, dr_idx, axis=1).transpose(0, 2, 1, 3)
        s_loc = jnp.einsum('bqhd,bikhd->bhqik', q_r, k_b).astype(jnp.float32) + bias[None].astype(jnp.float32)
        s_loc = jnp.where(col_valid[:, None, :], s_loc, -jnp.inf)
        s_ctx = jnp.einsum('bqhd,bchd->bhqc', q_r, kc).astype(jnp.float32)
        p = jax.nn.softmax(jnp.concatenate([s_loc.reshape(b, NA_HEADS, GRID_W, n_loc), s_ctx], axis=-1), axis=-1)
        p_loc = p[..., :n_loc].reshape(b, NA_HEADS, GRID_W, kh, GRID_W).astype(vg.dtype)
        p_ctx = p[..., n_loc:].astype(vc.dtype)
        return jnp.einsum('bhqik,bikhd->bqhd', p_loc, v_b) + jnp.einsum('bhqc,bchd->bqhd', p_ctx, vc)

    o = lax.map(row_block, jnp.arange(rows))
    y = o.transpose(1, 0, 2, 3, 4).reshape(b, s, d) @ w_out
    if not with_ctx_out:
        return y, None
    sc = jnp.einsum('bqhd,bkhd->bhqk', qc, kc).astype(jnp.float32)
    pc = jax.nn.softmax(sc, axis=-1).astype(vc.dtype)
    yc = jnp.einsum('bhqk,bkhd->bqhd', pc, vc).reshape(hc.shape) @ w_out
    return y, yc

def _conv_ffn(h, w_up, conv_w, conv_b, w_down):
    u = h @ w_up
    u = lax.conv_general_dilated(u, conv_w[:, None, :], window_strides=(1,),
                                 padding=[(CONV_W // 2, CONV_W // 2)],
                                 dimension_numbers=('NWC', 'WIO', 'NWC'),
                                 feature_group_count=u.shape[-1]) + conv_b
    a, g = jnp.split(u, 2, axis=-1)
    return (jax.nn.silu(a) * g) @ w_down

def setup_inputs(seed: int = 0) -> dict:
    key = jax.random.key(seed)
    ks = jax.random.split(key, 24)
    f32 = jnp.float32
    n_ret = (DEPTH + 1) // 2
    n_na = DEPTH // 2
    kh = min(NA_MAX_KH, SEQ // GRID_W)
    nrm = lambda k, shape, fan_in: jax.random.normal(k, shape, f32) * fan_in ** -0.5
    hk = RET_HEADS * RET_QK_DIM
    hv = RET_HEADS * RET_V_DIM
    dlog0 = jnp.asarray(np.log(-np.log(1.0 - 2.0 ** (-5.0 - np.arange(RET_HEADS)))).astype(np.float32))
    return {
        "x": jax.random.normal(ks[0], (BATCH, SEQ, D_MODEL), f32),
        "c": jax.random.normal(ks[1], (BATCH, D_MODEL), f32),
        "ctx": jax.random.normal(ks[2], (BATCH, CTX_LEN, D_MODEL), f32),
        "c_ctx": jax.random.normal(ks[3], (D_MODEL,), f32),
        "ada_w": nrm(ks[4], (DEPTH, D_MODEL, 6 * D_MODEL), D_MODEL),
        "ada_b": 0.02 * jax.random.normal(ks[5], (DEPTH, 6 * D_MODEL), f32),
        "norm1_w": 1.0 + 0.02 * jax.random.normal(ks[6], (DEPTH, D_MODEL), f32),
        "norm2_w": 1.0 + 0.02 * jax.random.normal(ks[7], (DEPTH, D_MODEL), f32),
        "ret_w_in": nrm(ks[8], (n_ret, D_MODEL, 2 * hk + 2 * hv), D_MODEL),
        "ret_decay_fwd": dlog0[None] + 0.01 * jax.random.normal(ks[9], (n_ret, RET_HEADS), f32),
        "ret_decay_bwd": dlog0[None] + 0.01 * jax.random.normal(ks[10], (n_ret, RET_HEADS), f32),
        "ret_w_out": nrm(ks[11], (n_ret, hv, D_MODEL), hv),
        "na_w_qkv": nrm(ks[12], (n_na, D_MODEL, 3 * D_MODEL), D_MODEL),
        "na_rpb": 0.02 * jax.random.normal(ks[13], (n_na, NA_HEADS, 2 * kh - 1, 2 * NA_KW - 1), f32),
        "na_w_out": nrm(ks[14], (n_na, D_MODEL, D_MODEL), D_MODEL),
        "ffn_w_up": nrm(ks[15], (DEPTH, D_MODEL, 2 * FFN_DIM), D_MODEL),
        "ffn_conv_w": nrm(ks[16], (DEPTH, CONV_W, 2 * FFN_DIM), CONV_W),
        "ffn_conv_b": 0.02 * jax.random.normal(ks[17], (DEPTH, 2 * FFN_DIM), f32),
        "ffn_w_down": nrm(ks[18], (DEPTH, FFN_DIM, D_MODEL), FFN_DIM),
        "final_norm_w": 1.0 + 0.02 * jax.random.normal(ks[19], (D_MODEL,), f32),
    }

def reference(x, c, ctx, c_ctx, ada_w, ada_b, norm1_w, norm2_w, ret_w_in, ret_decay_fwd, ret_decay_bwd,
              ret_w_out, na_w_qkv, na_rpb, na_w_out, ffn_w_up, ffn_conv_w, ffn_conv_b, ffn_w_down,
              final_norm_w):
    seq = x.shape[1]
    rows = seq // GRID_W
    t = jnp.arange(seq)
    pos_r = (t // GRID_W).astype(jnp.float32)
    pos_c = (t % GRID_W).astype(jnp.float32)
    sc = jax.nn.silu(c)
    sc_ctx = jax.nn.silu(c_ctx)
    for i in range(DEPTH):
        last = i == DEPTH - 1
        j = i // N_MIXERS
        sh1, sc1, g1, sh2, sc2, g2 = jnp.split((sc @ ada_w[i] + ada_b[i])[:, None, :], 6, axis=-1)
        csh1, csc1, cg1, csh2, csc2, cg2 = jnp.split(sc_ctx @ ada_w[i] + ada_b[i], 6, axis=-1)
        h = _modulate(_rmsnorm(x, norm1_w[i]), sh1, sc1)
        hc = _modulate(_rmsnorm(ctx, norm1_w[i]), csh1, csc1)
        if i % N_MIXERS == 0:
            y, yc = _retention(h, hc, ret_w_in[j], ret_decay_fwd[j], ret_decay_bwd[j], ret_w_out[j], pos_r, pos_c)
        else:
            y, yc = _neighbourhood_attention(h, hc, na_w_qkv[j], na_rpb[j], na_w_out[j], rows, not last)
        x = x + g1 * y
        h2 = _modulate(_rmsnorm(x, norm2_w[i]), sh2, sc2)
        x = x + g2 * _conv_ffn(h2, ffn_w_up[i], ffn_conv_w[i], ffn_conv_b[i], ffn_w_down[i])
        if not last:
            ctx = ctx + cg1 * yc
            hc2 = _modulate(_rmsnorm(ctx, norm2_w[i]), csh2, csc2)
            ctx = ctx + cg2 * _conv_ffn(hc2, ffn_w_up[i], ffn_conv_w[i], ffn_conv_b[i], ffn_w_down[i])
    return _rmsnorm(x, final_norm_w)


_drawn_inputs = setup_inputs


def setup_inputs(seed=0):
    import zlib

    import numpy as np

    out = dict(_drawn_inputs(seed))
    spreads = {}
    factors = {'norm1_w': 2.852,
     'norm2_w': 3.109,
     'na_rpb': 49.229,
     'ffn_conv_b': 3.662,
     'final_norm_w': 7.915}
    for name, (base, spread) in spreads.items():
        noise = np.random.default_rng([zlib.crc32(name.encode()), seed]).standard_normal(out[name].shape)
        drawn = base * np.exp(spread * noise) if base else spread * noise
        out[name] = __import__('jax').numpy.asarray(drawn.astype(out[name].dtype))
    for name, factor in factors.items():
        out[name] = (out[name] * factor).astype(out[name].dtype)
    return out
```

```python
from contextlib import ExitStack, contextmanager

import numpy as np
import concourse.bass as bass
from concourse import mybir

F32 = mybir.dt.float32
F32R = mybir.dt.float32r
ALU = mybir.AluOpType
ACT = mybir.ActivationFunctionType

P = 128
D = 1024
KC = D // P
LAT, CTX = 512, 256
TOK = LAT + CTX
ROWS, COLS = LAT // 64, 64
EPS = 1e-6
RH, RQK, RV = 4, 256, 512
VC = RV // P
TT = TOK // P
NH, ND, NKW = 16, 64, 16
NP = NH // 2
QB = 4
F = 2816
FC = F // P
GROUPS = (8, 8, 6)
OUT_SLOTS = 4
CHUNKS = RH * (12 + OUT_SLOTS) + 2 * (2 * FC + 8 * len(GROUPS)) + 3 * NP + 8
PARTS = ((0, LAT, 0), (LAT, CTX, 1))
WIN = ((0, 24), (8, 32), (24, 32), (40, 24))
TILES = ((0, 2), (0, 3), (1, 3), (2, 2))
MASKS = (0, 1, 1, 2)
SMALL = (("cond", 16), ("norm_w", 40), ("ada_b", 96), ("dlog", 8), ("cos_r", 8), ("sin_r", 8),
         ("cos_c", 64), ("sin_c", 64), ("conv", 2 * FC * 8), ("ident", P))
NSMALL = sum(n for _, n in SMALL)


class Tally:

    def __init__(self):
        self.base, self.n = 0, 0

    def now(self):
        return self.base + self.n if self.n else self.base

    def up(self, k=1):
        self.n += k
        return self.now()

    def began(self):
        return not (isinstance(self.base, int) and self.base + self.n == 0)


@contextmanager
def turns(eng, trips, steps):
    was = [(t, t.base, t.n) for t, _ in steps]
    with eng.Fori(0, trips) as i:
        for t, k in steps:
            t.base, t.n = eng.snap(i * k + t.now()), 0
        yield i
        left = [(j, t.n, k) for j, (t, k) in enumerate(steps) if t.n != k]
        assert not left, f"tallies (index, made, promised): {left}"
    for (t, base, n), (_, k) in zip(was, steps):
        t.base, t.n = base, n + trips * k


class AccLine:

    def __init__(self):
        self.full, self.taken, self.turn = Tally(), (Tally(), Tally()), 0

    def next(self, counted=True):
        i = self.turn
        self.turn = 1 - i
        full = self.full.up() if counted else None
        began = self.taken[i].began()
        before = self.taken[i].now()
        return i, full, (before if began else None), self.taken[i].up()

    def next_at(self, i):
        turn, self.turn = self.turn, i
        got = self.next()
        self.turn = turn
        return got

    def steps(self, tiles, extra0=0):
        assert tiles % 2 == 0
        return [(self.full, tiles + extra0), (self.taken[0], tiles // 2 + extra0), (self.taken[1], tiles // 2)]


def backbone(nc, x_in, weights, ada_first, ada, cond_rows, small_in, bias_in, masks_in, park, out):
    ctx = ExitStack()
    with ctx:
        def sem(name):
            return ctx.enter_context(nc.semaphore(name))

        def sb(name, shape, dt=F32, stack=ctx):
            return stack.enter_context(nc.sbuf_tensor(name, shape, dt))

        with ExitStack() as part:
            x = sb("x", [P, KC, TOK], stack=part)
        pt_hi = sb("pt_hi", [P, TT, QB * P], F32R)
        pt_lo = sb("pt_lo", [P, TT, QB * P], F32R)
        h_hi = sb("h_hi", [P, KC, TOK], F32R)
        h_lo = sb("h_lo", [P, KC, TOK], F32R)
        raw = [sb(f"raw{i}", [P, D]) for i in range(2)]
        w_hi = [sb(f"w_hi{i}", [P, D], F32R) for i in range(2)]
        w_lo = [sb(f"w_lo{i}", [P, D], F32R) for i in range(2)]
        small = sb("small", [P, NSMALL])
        mod = sb("mod", [P, 2, 48, 2])
        norm_a = sb("norm_a", [P, KC, 2])
        silu_c = sb("silu_c", [P, KC, 2])
        ones = sb("ones", [P, P])
        ss = sb("ss", [P, TOK])
        S = [sb(f"scratch{i}", [P, 1024 if i == 3 else 896]) for i in range(4)]
        mod_new = sb("mod_new", [P, 8, 2])
        at, cols = 0, {}
        for name, n in SMALL:
            cols[name] = small[:, at:at + n]
            at += n
        cond = cols["cond"].rearrange("p (k c) -> p k c", c=2)
        norm_w = cols["norm_w"].rearrange("p (n k) -> p n k", k=KC)
        ada_b = cols["ada_b"].rearrange("p (l j) -> p l j", l=2)
        conv = cols["conv"].rearrange("p (l f c) -> p l f c", l=2, c=8)
        ident = cols["ident"]

        with ExitStack() as stage:
            ada_raw = sb("ada_raw", [P, D], stack=stage)
            silu_rows = sb("silu_rows", [P, 2, D], stack=stage)
            with ExitStack() as part:
                ada_start = [sb(f"ada_start{i}", [P, 4, D], stack=part) for i in range(4)]
            with ExitStack() as part:
                qk_hi = sb("qk_hi", [P, 4, TOK], F32R, part)
                qk_lo = sb("qk_lo", [P, 4, TOK], F32R, part)
                vg_hi = sb("vg_hi", [P, VC * TOK], F32R, part)
                vg_lo = sb("vg_lo", [P, VC * TOK], F32R, part)
                vo = sb("vo", [P, VC, TOK], stack=part)
                p_hi = [sb(f"p_hi{i}", [P, LAT], F32R, part) for i in range(2)]
                p_lo = [sb(f"p_lo{i}", [P, LAT], F32R, part) for i in range(2)]
                dist = sb("dist", [P, 896], stack=part)
                near = sb("near", [P, 896], stack=part)
                far = sb("far", [P, 640], stack=part)
                logs = sb("logs", [P, RH, 8], stack=part)
                head_logs = sb("head_logs", [P, 8], stack=part)
            with ExitStack() as part:
                act_hi = sb("act_hi", [P, 8, TOK], F32R, part)
                act_lo = sb("act_lo", [P, 8, TOK], F32R, part)
                u = [sb(f"u{i}", [P, TOK + 4], stack=part) for i in range(2)]
                taps = sb("taps", [P, 8], stack=part)
                waste = sb("waste", [P, D], stack=part)
        with ExitStack() as stage:
            masks = sb("masks", [P, 3, 256], stack=stage)
            rel = [sb(f"rel{i}", [P, 256], stack=stage) for i in range(2)]
            nq = sb("nq", [P, 2, LAT], F32R, stage)
            nk_hi = sb("nk_hi", [P, 2, TOK], F32R, stage)
            nk_lo = sb("nk_lo", [P, 2, TOK], F32R, stage)
            nv_hi = sb("nv_hi", [P, TT, 2, P], F32R, stage)
            nv_lo = sb("nv_lo", [P, TT, 2, P], F32R, stage)
            prob = [sb(f"prob{a}", [P, TILES[a][1] * P + CTX], stack=stage) for a in range(QB)]
            bias = [sb(f"bias{i}", [P, 3, LAT], stack=stage) for i in range(2)]
            no_hi = sb("no_hi", [P, NP, LAT], F32R, stage)
            no_lo = sb("no_lo", [P, NP, LAT], F32R, stage)
            top = sb("top", [P, 2, 8], stack=stage)

        acc = [ctx.enter_context(nc.psum_tensor(f"acc{i}", [P, 2 * LAT], F32)) for i in range(2)]
        o_ps = ctx.enter_context(nc.psum_tensor("o_ps", [P, VC, LAT], F32))
        side = [o_ps[:, 2 * i:2 * i + 2, :].rearrange("p a t -> p (a t)") for i in range(2)]

        acc_full = sem("acc_full")
        acc_taken = [sem("acc_taken0"), sem("acc_taken1")]
        const_in, x_loaded, masks_loaded = sem("const_in"), sem("x_loaded"), sem("masks_loaded")
        raw_in = [sem("raw_in0"), sem("raw_in1")]
        hi_split, lo_split = sem("hi_split"), sem("lo_split")
        ada_start_in = [sem(f"ada_start_in{i}") for i in range(4)]
        rows_in, ada_in, ada_used, ada_started = sem("rows_in"), sem("ada_in"), sem("ada_used"), sem("ada_started")
        side_full, side_taken = sem("side_full"), [sem("side_taken0"), sem("side_taken1")]
        set_up = sem("set_up")
        cond_done = sem("cond_done")
        vec_step = sem("vec_step")
        sq_done, sq_added = sem("sq_done"), sem("sq_added")
        norm_t, h_hi_done, h_lo_done = sem("norm_t"), sem("h_hi_done"), sem("h_lo_done")
        dist_ready, decay_exp = sem("dist_ready"), sem("decay_exp")
        v_hi_done = sem("v_hi_done")
        rope_done, qk_hi_done = sem("rope_done"), sem("qk_hi_done")
        p_hi_done, p_lo_done, pv_done, o_taken = sem("p_hi_done"), sem("p_lo_done"), sem("pv_done"), sem("o_taken")
        gate_mul, gate_hi, gate_lo = sem("gate_mul"), sem("gate_hi"), sem("gate_lo")
        conv_done, silu_done, act_mul = sem("conv_done"), sem("silu_done"), sem("act_mul")
        act_hi_done, act_lo_done = sem("act_hi_done"), sem("act_lo_done")
        rel_in, bias_done, parked, x_back = sem("rel_in"), sem("bias_done"), sem("parked"), sem("x_back")
        n_hi_done = sem("n_hi_done")
        s_full, s_taken, max_done, exp_done = sem("s_full"), sem("s_taken"), sem("max_done"), sem("exp_done")
        sum_done, prob_done, pt_hi_done = sem("sum_done"), sem("prob_done"), sem("pt_hi_done")
        npv_done, no_taken = sem("npv_done"), sem("no_taken")
        x_ready, x_out = sem("x_ready"), sem("x_out")

        SCORES = [(LAT + P * j, LAT, CTX, near, 384 - P * j, 4 + j) for j in range(2)]
        SCORES += [(P * j, 0, LAT, near, 384 - P * j, j) for j in range(4)]
        SCORES += [(LAT + P * j, 0, LAT, far, P - P * j, 4 + j) for j in range(2)]
        HEAD_CHUNKS = 12
        HEAD_TILES = 4 + 4 + 8 + 4
        HEAD_SIDE = 4

        block = ctx.enter_context(nc.Block())

        @block.sync
        def _(sp):
            sp.dma_start(small[:, :], small_in).then_inc(const_in, 16)
            for i in range(4):
                sp.dma_start(ada_start[i][:, :, :], ada_first[4 * i:4 * i + 4, :, :].rearrange("a p n -> p a n"))\
                  .then_inc(ada_start_in[i], 16)
                if i == 0:
                    sp.dma_start(x[:, :, :], x_in).then_inc(x_loaded, 16)
            for c in range(2):
                sp.dma_start(silu_rows[:, c, :], cond_rows[c, :].partition_broadcast(P)).then_inc(rows_in, 16)
            sp.dma_start(raw[0][:, :], weights[0, :, :]).then_inc(raw_in[0], 16)
            sp.dma_start(raw[1][:, :], weights[1, :, :]).then_inc(raw_in[1], 16)
            with sp.Fori(1, CHUNKS // 2) as i:
                for slot in range(2):
                    sp.wait_ge(lo_split, i * 2 + (slot - 1))
                    sp.dma_start(raw[slot][:, :], weights[bass.ds(i * 2 + slot, 1), :, :].rearrange("a p n -> p (a n)"))\
                      .then_inc(raw_in[slot], 16)
            for k in range(KC):
                sp.wait_ge(x_ready, k + 1)
                sp.dma_start(out[:, k, :], x[:, k, 0:LAT]).then_inc(x_out, 16)
            sp.wait_ge(x_out, 16 * KC)

        @block.gpsimd
        def _(pool):
            pool.dma_start(ada_raw[:, :], ada[0, :, :]).then_inc(ada_in, 16)
            nc.gpsimd.memset(ones[:, :], 1.0).then_inc(set_up, 1)
            nc.gpsimd.iota(dist[:, :], pattern=[[1, 896]], base=-384, channel_multiplier=-1,
                           allow_small_or_imprecise_dtypes=True).then_inc(set_up, 1)
            with pool.Fori(1, 80) as i:
                pool.wait_ge(ada_used, i)
                pool.dma_start(ada_raw[:, :], ada[bass.ds(i, 1), :, :].rearrange("a p n -> p (a n)")).then_inc(ada_in, 16)

            pool.wait_ge(sq_done, 2 * KC + RH * VC + 1)
            pool.dma_start(masks[:, :, :], masks_in).then_inc(masks_loaded, 16)
            zeros = [nv_hi[:, :, :, :].bitcast(F32), nv_lo[:, :, :, :].bitcast(F32)] + [prob[a][:, :] for a in range(QB)]
            zeros += [bias[i][:, :, :] for i in range(2)]
            for z in zeros:
                nc.gpsimd.memset(z, 0.0).then_inc(set_up, 1)
            pool.wait_ge(norm_t, 3 * KC)
            pool.dma_start(park, x[:, :, 0:LAT]).then_inc(parked, 16)

            rels, biases, taken, sums = Tally(), Tally(), Tally(), Tally()

            def load_rel(c, hh):
                pool.dma_start(rel[hh][:, :], bias_in[bass.ds(c * 2 + hh, 1), :, :].rearrange("a p n -> p (a n)"))\
                    .then_inc(rel_in, 16)

            def make_bias(hh):
                for m, (lo, n) in enumerate(((64, 192), (0, 256), (0, 192))):
                    nc.gpsimd.tensor_tensor(bias[hh][:, m, 0:n], rel[hh][:, lo:lo + n], masks[:, m, lo:lo + n], ALU.add)\
                        .then_inc(bias_done, 1)
                biases.up(3)

            def scale_probs(blocks):
                for i in blocks:
                    pool.wait_ge(sum_done, sums.up())
                    n = TILES[i % QB][1] * P + CTX
                    nc.gpsimd.tensor_tensor(prob[i % QB][:, :], prob[i % QB][:, :], top[:, i % 2, 4:5].to_broadcast([P, n]), ALU.mult)\
                        .then_inc(prob_done, 1)

            load_rel(0, 0)
            load_rel(0, 1)
            pool.wait_ge(masks_loaded, 16)
            pool.wait_ge(set_up, 2 + len(zeros))
            pool.wait_ge(rel_in, rels.up(32))
            make_bias(0)
            make_bias(1)
            with turns(pool, NP - 1, [(rels, 32), (biases, 6), (taken, 8), (sums, 8)]) as c:
                pool.wait_ge(bias_done, biases.now())
                load_rel(c + 1, 0)
                load_rel(c + 1, 1)
                pool.wait_ge(rel_in, rels.up(32))
                for hh in range(2):
                    scale_probs(range(4 * hh, 4 * hh + 4))
                    pool.wait_ge(s_taken, taken.up(4) + 1)
                    make_bias(hh)
            scale_probs(range(8))
            pool.wait_ge(npv_done, 2 * NP)
            pool.wait_ge(parked, 16)
            pool.dma_start(x[:, :, 0:LAT], park).then_inc(x_back, 16)

        @block.tensor
        def _(pe):
            A, B = AccLine(), AccLine()
            chunk = Tally()
            sq, h, pl, ot, gl, al = Tally(), Tally(), Tally(), Tally(), Tally(), Tally()
            slot, opened, value_tiles = [0], [None], {}

            def open_acc(counted=True):
                i, _, before, after = A.next(counted)
                if before is not None:
                    pe.wait_ge(acc_taken[i], before)
                opened[0] = (i, after)
                return acc[i]

            def open_side(got):
                i, _, before, after = got
                if before is not None:
                    pe.wait_ge(side_taken[i], before)
                return side[i]

            def next_chunk():
                pe.wait_ge(lo_split, chunk.up())
                i = slot[0]
                slot[0] = 1 - i
                return w_hi[i], w_lo[i]

            def product(tile, w, blocks, hi, lo, parts, ready=None):
                last = len(blocks) - 1
                for n, b in enumerate(blocks):
                    if ready is not None:
                        ready(n)
                    for m, (wt, mv) in enumerate(((w[0], hi), (w[0], lo), (w[1], hi))):
                        for c0, cn, _ in parts:
                            mm = nc.tensor.matmul(tile[:, c0:c0 + cn], wt[:, b * P:(b + 1) * P], mv[:, n, c0:c0 + cn],
                                                  start=(n == 0 and m == 0), stop=(n == last and m == 2))
                mm.then_inc(acc_full, 1)

            def project(hi, lo, parts, ready=None):
                w = next_chunk()
                product(open_acc(), w, range(KC), hi, lo, parts, ready)

            def start_ada():
                tile = open_acc(counted=False)
                for i in range(4):
                    pe.wait_ge(ada_start_in[i], 16)
                    for j in range(4):
                        at = 2 * (4 * i + j)
                        for k in range(KC):
                            mm = nc.tensor.matmul(tile[:, at:at + 2], ada_start[i][:, j, k * P:(k + 1) * P],
                                                  silu_c[:, k, :], start=(k == 0), stop=(k == KC - 1))
                mm.then_inc(ada_started, 1)

            def ones_tile(n, parts, on_side=False):
                pe.wait_ge(sq_added, sq.up(n))
                tile = open_side(B.next_at(0)) if on_side else open_acc()
                for c0, cn, _ in parts:
                    mm = nc.tensor.matmul(tile[:, c0:c0 + cn], ones[:, :], ss[:, c0:c0 + cn], start=True, stop=True)
                mm.then_inc(side_full if on_side else acc_full, 1)

            def h_ready(first):
                return lambda n: pe.wait_ge(h_lo_done, first + n + 1)

            def head_front(hd, first):
                ready = None
                if first:
                    ready = h_ready(h.now())
                    h.up(KC)
                project(h_hi, h_lo, PARTS, ready)
                value_tiles[0] = opened[0]
                project(h_hi, h_lo, PARTS)
                value_tiles[1] = opened[0]
                if not first:
                    out_projection()
                turn_values(0)
                project(h_hi, h_lo, PARTS)
                value_tiles[2] = opened[0]
                turn_values(1)
                project(h_hi, h_lo, PARTS)
                value_tiles[3] = opened[0]
                turn_values(2)
                project(h_hi, h_lo, PARTS)
                turn_values(3)
                for _ in range(3):
                    project(h_hi, h_lo, PARTS)

            def turn_values(vc):
                i, after = value_tiles[vc]
                pe.wait_ge(acc_taken[i], after)
                tile = open_side(B.next())
                for t in range(TT):
                    mm = nc.tensor.transpose(tile[:, t * P:(t + 1) * P], vo[:, vc, t * P:(t + 1) * P], ident)
                mm.then_inc(side_full, 1)

            def scores(i):
                k0, q0, qn, _, _, _ = SCORES[i]
                tile = open_acc()
                for d in range(2):
                    for m, (kt, qt) in enumerate(((qk_hi, qk_hi), (qk_hi, qk_lo), (qk_lo, qk_hi))):
                        mm = nc.tensor.matmul(tile[:, 0:qn], kt[:, d, k0:k0 + P], qt[:, 2 + d, q0:q0 + qn],
                                              start=(d == 0 and m == 0), stop=(d == 1 and m == 2))
                mm.then_inc(acc_full, 1)

            def values(tiles, first, last):
                for vc in range(VC):
                    for n, i in enumerate(tiles):
                        _, _, qn, _, _, t = SCORES[i]
                        c0 = t * RV + vc * P
                        for m, (vt, pt) in enumerate(((vg_hi, p_hi), (vg_hi, p_lo), (vg_lo, p_hi))):
                            mm = nc.tensor.matmul(o_ps[:, vc, 0:qn], vt[:, c0:c0 + P], pt[i % 2][:, 0:qn],
                                                  start=(first and n == 0 and m == 0),
                                                  stop=(last and n == len(tiles) - 1 and m == 2))
                mm.then_inc(pv_done, 1)

            def head_attention():
                pe.wait_ge(acc_taken[0], A.taken[0].now())
                pe.wait_ge(acc_taken[1], A.taken[1].now())
                scores(0)
                scores(1)
                scores(2)
                pe.wait_ge(p_lo_done, pl.up(2))
                for i in range(2):
                    pe.wait_ge(side_taken[i], B.taken[i].now())
                values((0, 1), True, True)
                pe.wait_ge(o_taken, ot.up())
                for i in range(2, 8):
                    if i < 7:
                        scores(i + 1)
                    pe.wait_ge(p_lo_done, pl.up())
                    values((i,), i == 2, i == 7)
                ot.up()
                project(h_hi, h_lo, PARTS)
                project(h_hi, h_lo, PARTS)
                ones_tile(VC, PARTS, on_side=True)
                project(h_hi, h_lo, PARTS)
                project(h_hi, h_lo, PARTS)

            def out_projection():
                pe.wait_ge(gate_lo, gl.up(VC))
                hi = vg_hi[:, :].rearrange("p (k t) -> p k t", k=VC)
                lo = vg_lo[:, :].rearrange("p (k t) -> p k t", k=VC)
                for _ in range(OUT_SLOTS):
                    w = next_chunk()
                    for m in range(2):
                        product(open_acc(), w, range(m * VC, (m + 1) * VC), hi, lo, PARTS)

            def ffn(parts):
                ready = h_ready(h.now())
                first = True
                for size in GROUPS:
                    at = al.now()

                    def act_ready(n):
                        pe.wait_ge(act_lo_done, at + n + 1)

                    if first:
                        h.up(KC)
                    with turns(pe, size, A.steps(2) + [(chunk, 2)]):
                        project(h_hi, h_lo, parts, ready if first else None)
                        project(h_hi, h_lo, parts)
                    first = False
                    al.up(size)
                    with turns(pe, 4, A.steps(2) + [(chunk, 2)]):
                        for m in range(2):
                            w = next_chunk()
                            product(open_acc(), w, range(size), act_hi, act_lo, parts, act_ready if m == 0 else None)

            st, pn, npv = Tally(), Tally(), Tally()

            def block_scores(i):
                hh, a = divmod(i, QB)
                pe.wait_ge(s_taken, st.now() + max(i, 1))
                tile = o_ps[:, 1 + i % 2, :]
                q = nq[:, hh, a * P:(a + 1) * P]
                w0, wn = WIN[a][0] * ROWS, WIN[a][1] * ROWS
                for c0, k0, n in ((0, w0, wn), (wn, LAT, CTX)):
                    for m, nk in enumerate((nk_hi, nk_lo)):
                        mm = nc.tensor.matmul(tile[:, c0:c0 + n], q, nk[:, hh, k0:k0 + n], start=(m == 0), stop=(m == 1))
                mm.then_inc(s_full, 1)

            def turn_probs(i):
                a = i % QB
                pe.wait_ge(prob_done, pn.up())
                tile = open_acc()
                for t in range(TILES[a][1] + 2):
                    mm = nc.tensor.transpose(tile[:, t * P:(t + 1) * P], prob[a][:, t * P:(t + 1) * P], ident)
                mm.then_inc(acc_full, 1)

            def pair_values(hh):
                pe.wait_ge(acc_taken[0], A.taken[0].now())
                pe.wait_ge(acc_taken[1], A.taken[1].now())
                if hh == 0:
                    pe.wait_ge(no_taken, npv.now() + 1)
                for n, t in enumerate((4, 5, 0, 1, 2, 3)):
                    a0, a1 = (0, QB) if t >= 4 else (max(0, t - 1), min(QB, t + 2))
                    for m, (vt, pt) in enumerate(((nv_hi, pt_hi), (nv_hi, pt_lo), (nv_lo, pt_hi))):
                        mm = nc.tensor.matmul(o_ps[:, 0, a0 * P:a1 * P], vt[:, t, hh, :], pt[:, t, a0 * P:a1 * P],
                                              start=(hh == 0 and n == 0 and m == 0),
                                              stop=(hh == 1 and n == 5 and m == 2))
                mm.then_inc(npv_done, 1)

            LATENT = PARTS[:1]

            def pair(ready):
                project(h_hi, h_lo, LATENT, ready)
                project(h_hi, h_lo, PARTS)
                project(h_hi, h_lo, PARTS)
                i, after = opened[0]
                pe.wait_ge(acc_taken[i], after)
                tile = open_acc()
                for t in range(TT):
                    mm = nc.tensor.transpose(tile[:, t * P:(t + 1) * P], S[2][:, t * P:(t + 1) * P], ident)
                mm.then_inc(acc_full, 1)
                pe.wait_ge(acc_taken[0], A.taken[0].now())
                pe.wait_ge(acc_taken[1], A.taken[1].now())
                block_scores(0)
                block_scores(1)
                for i in range(8):
                    if i + 2 < 8:
                        block_scores(i + 2)
                    if i == 4:
                        pair_values(0)
                    turn_probs(i)
                pair_values(1)
                st.up(8)
                npv.up()

            pe.wait_ge(cond_done, 1)
            start_ada()
            pe.wait_ge(set_up, 1)
            ones_tile(KC, PARTS)
            head_front(0, True)
            head_attention()
            with turns(pe, RH - 1, A.steps(HEAD_TILES + 8) + B.steps(HEAD_SIDE, 1) + [(chunk, 16), (sq, VC), (pl, 8), (ot, 2),
                                                                                     (gl, VC)]):
                head_front(None, False)
                head_attention()
            out_projection()
            ones_tile(KC, PARTS)
            ffn(PARTS)
            ones_tile(KC, PARTS)
            pe.wait_ge(set_up, 10)
            ready = h_ready(h.now())
            with turns(pe, NP // 2, A.steps(24) + [(chunk, 6), (st, 16), (pn, 16), (npv, 2)]):
                for _ in range(2):
                    pair(ready)
            h.up(KC)
            pe.wait_ge(no_taken, NP + 1)
            with turns(pe, 4, A.steps(2) + [(chunk, 2)]):
                for _ in range(2):
                    project(no_hi, no_lo, LATENT)
            ones_tile(KC, LATENT)
            ffn(LATENT)
            ones_tile(KC, LATENT)

        @block.scalar
        def _(act):
            A, B = AccLine(), AccLine()
            raws, slot = [Tally(), Tally()], [0]
            sqa, nt, dx, rp, pl, pv, ot = Tally(), Tally(), Tally(), Tally(), Tally(), Tally(), Tally()
            gm, gl, cd, am, de = Tally(), Tally(), Tally(), Tally(), Tally()

            def split():
                i = slot[0]
                slot[0] = 1 - i
                act.wait_ge(raw_in[i], raws[i].up(16))
                nc.scalar.activation(w_hi[i][:, :], raw[i][:, :], ACT.Copy).then_inc(hi_split, 1)

            def wait_full():
                i, full, _, after = A.next()
                act.wait_ge(acc_full, full)
                return i, acc[i]

            def wait_side(got):
                i, full, _, _ = got
                act.wait_ge(side_full, full)
                return i, side[i]

            def squares(src, n, width):
                for k in range(n):
                    if k >= 2:
                        act.wait_ge(sq_added, sqa.now() + k - 1)
                    nc.scalar.activation(S[k % 2][:, 0:width], src[:, k, 0:width], ACT.Square).then_inc(sq_done, 1)
                sqa.up(n)

            def root(n, width, on_side=False):
                i, tile = wait_side(B.next_at(0)) if on_side else wait_full()
                nc.scalar.activation(ss[:, 0:width], tile[:, 0:width], ACT.Sqrt, bias=EPS, scale=1.0 / n)\
                  .then_inc((side_taken if on_side else acc_taken)[i], 1)

            def x_final():
                act.wait_ge(acc_taken[0], A.taken[0].now())
                act.wait_ge(acc_taken[1], A.taken[1].now())

            def norm(layer, shift, parts):
                width = TOK if len(parts) > 1 else LAT
                squares(x, KC, width)
                root(D, width)
                for k in range(KC):
                    act.wait_ge(norm_t, nt.up())
                    for c0, cn, c in parts:
                        ins = nc.scalar.activation(h_hi[:, k, c0:c0 + cn], S[2 + k % 2][:, c0:c0 + cn], ACT.Identity,
                                                   bias=mod[:, layer, shift + k, c:c + 1], scale=norm_a[:, k, c:c + 1])
                    ins.then_inc(h_hi_done, 1)

            def take_value(vc):
                i, tile = wait_full()
                nc.scalar.activation(vo[:, vc, :], tile[:, 0:TOK], ACT.Copy).then_inc(acc_taken[i], 1)
                split()

            def value_hi(vc):
                i, tile = wait_side(B.next())
                out_v = vg_hi[:, :].rearrange("p (t v) -> p t v", v=RV)[:, :, vc * P:(vc + 1) * P]
                nc.scalar.activation(out_v, tile[:, 0:TOK].rearrange("p (t v) -> p t v", v=P), ACT.Copy)\
                  .then_inc(v_hi_done, 1)

            def key_hi(j):
                i, tile = wait_full()
                nc.scalar.activation(qk_hi[:, j, LAT:TOK], tile[:, LAT:TOK], ACT.Copy).then_inc(qk_hi_done, 1)
                split()
                act.wait_ge(rope_done, rp.up())
                nc.scalar.activation(qk_hi[:, j, 0:LAT], S[2][:, 0:LAT], ACT.Copy).then_inc(qk_hi_done, 1)

            def head_front(first):
                if not first:
                    act.wait_ge(gate_lo, gl.now())
                take_value(0)
                act.wait_ge(dist_ready, dx.up())
                nc.scalar.activation(near[:, :], S[0][:, :], ACT.Exp, scale=head_logs[:, 0:1]).then_inc(decay_exp, 1)
                nc.scalar.activation(S[1][:, :], S[1][:, :], ACT.Exp, scale=head_logs[:, 1:2]).then_inc(decay_exp, 1)
                nc.scalar.activation(far[:, :], dist[:, 0:640], ACT.Exp, scale=head_logs[:, 0:1], bias=head_logs[:, 2:3])\
                  .then_inc(decay_exp, 1)
                act.wait_ge(decay_exp, de.up())
                de.up(3)
                nc.scalar.activation(S[0][:, 0:640], dist[:, 0:640], ACT.Exp, scale=head_logs[:, 3:4], bias=head_logs[:, 4:5])\
                  .then_inc(decay_exp, 1)
                take_value(1)
                if not first:
                    for _ in range(OUT_SLOTS):
                        wait_full()
                        wait_full()
                        split()
                value_hi(0)
                take_value(2)
                value_hi(1)
                take_value(3)
                value_hi(2)
                key_hi(0)
                value_hi(3)
                for j in range(1, 4):
                    key_hi(j)

            def head_attention():
                v0, g0 = pv.now(), gm
                for i in range(8):
                    qn = SCORES[i][2]
                    t, _, _, after = A.next()
                    act.wait_ge(acc_taken[t], after)
                    if i == 2:
                        act.wait_ge(pv_done, v0 + 1)
                        nc.scalar.activation(vo[:, :, LAT:TOK], o_ps[:, :, 0:CTX], ACT.Copy).then_inc(o_taken, 1)
                    elif i > 3:
                        act.wait_ge(pv_done, v0 + (i - 2))
                    nc.scalar.activation(p_hi[i % 2][:, 0:qn], S[i % 2][:, 0:qn], ACT.Copy).then_inc(p_hi_done, 1)
                act.wait_ge(pv_done, pv.up(7))
                nc.scalar.activation(vo[:, :, 0:LAT], o_ps[:, :, :], ACT.Copy).then_inc(o_taken, 1)
                act.wait_ge(p_lo_done, pl.up(8))
                act.wait_ge(o_taken, ot.up(2))
                squares(vo, VC, TOK)
                for g in range(2):
                    i, tile = wait_full()
                    nc.scalar.activation(S[2 + g][:, 0:TOK], tile[:, 0:TOK], ACT.Silu).then_inc(acc_taken[i], 1)
                    split()
                root(RV, TOK, on_side=True)

                def gated_hi(g):
                    act.wait_ge(gate_mul, gm.up())
                    nc.scalar.activation(vg_hi[:, g * TOK:(g + 1) * TOK], vo[:, g, :], ACT.Copy).then_inc(gate_hi, 1)

                gated_hi(0)
                for g in range(2, 4):
                    i, tile = wait_full()
                    if g == 3:
                        gated_hi(1)
                    nc.scalar.activation(S[g][:, 0:TOK], tile[:, 0:TOK], ACT.Silu).then_inc(acc_taken[i], 1)
                    split()
                gated_hi(2)
                gated_hi(3)
                gl.up(4)

            def ffn(layer, parts, ends):
                for n, size in enumerate(GROUPS):
                    with turns(act, size, A.steps(2) + [(raws[0], 16), (raws[1], 16), (cd, 2), (am, 1)]) as f:
                        for j in range(2):
                            i, tile = wait_full()
                            if j == 0:
                                act.wait_ge(conv_done, cd.now() + (layer + 1))
                            for c0, cn, c in parts:
                                ins = nc.scalar.activation(u[j][:, c0 + c + 1:c0 + c + 1 + cn], tile[:, c0:c0 + cn], ACT.Copy)
                            ins.then_inc(acc_taken[i], 1)
                            split()
                            if j == 0:
                                act.wait_ge(conv_done, cd.now() + (layer + 2))
                                nc.scalar.activation(S[2][:, 0:TOK + 1], S[0][:, 0:TOK + 1], ACT.Silu).then_inc(silu_done, 1)
                        cd.up(2)
                        act.wait_ge(act_mul, am.up())
                        width = parts[-1][0] + parts[-1][1]
                        nc.scalar.activation(act_hi[:, bass.ds(f, 1), 0:width].rearrange("p a t -> p (a t)"),
                                             S[3][:, 0:width], ACT.Copy).then_inc(act_hi_done, 1)
                    pairs = 3 if ends and n == 2 else 4
                    with turns(act, pairs, A.steps(2) + [(raws[0], 16), (raws[1], 16)]):
                        for m in range(2):
                            wait_full()
                            split()
                    if pairs == 3:
                        A.next()
                        A.next()

            act.wait_ge(const_in, 16)
            nc.scalar.activation(silu_c[:, :, :], cond, ACT.Silu).then_inc(cond_done, 1)
            nc.scalar.activation(logs[:, :, 0:2], cols["dlog"].rearrange("p (h c) -> p h c", c=2), ACT.Exp)\
              .then_inc(cond_done, 1)
            act.wait_ge(rows_in, 32)
            nc.scalar.activation(silu_rows[:, :, :], silu_rows[:, :, :], ACT.Silu).then_inc(cond_done, 1)
            for _ in range(2):
                split()
            A.next(counted=False)
            act.wait_ge(x_loaded, 16)
            norm(0, 0, PARTS)
            head_front(True)
            head_attention()
            gl_steps = [(raws[0], 128), (raws[1], 128), (sqa, VC), (dx, 1), (de, 4), (rp, 4), (pl, 8), (pv, 7), (ot, 2), (gm, 4), (gl, 4)]
            with turns(act, RH - 1, A.steps(HEAD_TILES + 8) + B.steps(HEAD_SIDE, 1) + gl_steps):
                head_front(False)
                head_attention()
            for _ in range(OUT_SLOTS):
                wait_full()
                wait_full()
                split()
            x_final()
            norm(0, 24, PARTS)
            ffn(0, PARTS, False)
            x_final()
            norm(1, 0, PARTS)
            sf, mx, sd, npv = Tally(), Tally(), Tally(), Tally()

            def exps(i):
                hh, a = divmod(i, QB)
                wn = WIN[a][1] * ROWS
                c0 = WIN[a][0] * ROWS - TILES[a][0] * P
                c1 = TILES[a][1] * P
                act.wait_ge(max_done, mx.up())
                nc.scalar.activation(prob[a][:, c0:c0 + wn], S[i % 2][:, 0:wn], ACT.Exp, bias=top[:, i % 2, 1:2],
                                     accum_out=top[:, i % 2, 2:3])
                nc.scalar.activation(prob[a][:, c1:c1 + CTX], S[i % 2][:, wn:wn + CTX], ACT.Exp, bias=top[:, i % 2, 1:2],
                                     accum_out=top[:, i % 2, 3:4]).then_inc(exp_done, 1)

            def probs_hi(i):
                a = i % QB
                t, tile = wait_full()
                if i == 4:
                    act.wait_ge(npv_done, npv.now() + 1)
                t0, tn = TILES[a]
                nc.scalar.activation(pt_hi[:, t0:t0 + tn, a * P:(a + 1) * P],
                                     tile[:, 0:tn * P].rearrange("p (t q) -> p t q", q=P), ACT.Copy)
                nc.scalar.activation(pt_hi[:, 4:6, a * P:(a + 1) * P],
                                     tile[:, tn * P:(tn + 2) * P].rearrange("p (t q) -> p t q", q=P), ACT.Copy)\
                  .then_inc(pt_hi_done, 1)

            def pair(c):
                t, tile = wait_full()
                for hh in range(2):
                    nc.scalar.activation(nq[0:ND, hh, :], tile[hh * ND:(hh + 1) * ND, 0:LAT], ACT.Copy, scale=ND ** -0.5)\
                      .then_inc(n_hi_done, 1)
                split()
                t, tile = wait_full()
                for hh in range(2):
                    for half in range(2):
                        nc.scalar.activation(nk_hi[half * ND:(half + 1) * ND, hh, :], tile[hh * ND:(hh + 1) * ND, 0:TOK],
                                             ACT.Copy).then_inc(n_hi_done, 1)
                split()
                t, tile = wait_full()
                nc.scalar.activation(S[2][:, 0:TOK], tile[:, 0:TOK], ACT.Copy).then_inc(acc_taken[t], 1)
                split()
                t, tile = wait_full()
                for hh in range(2):
                    own = slice(hh * ND, (hh + 1) * ND)
                    nc.scalar.activation(nv_hi[:, :, hh, own], tile[:, 0:TOK].rearrange("p (t v) -> p t v", v=P)[:, :, own],
                                         ACT.Copy).then_inc(n_hi_done, 1)
                act.wait_ge(parked, 16)
                exps(0)
                exps(1)
                for i in range(8):
                    if i + 2 < 8:
                        exps(i + 2)
                    probs_hi(i)
                act.wait_ge(npv_done, npv.up(2))
                nc.scalar.activation(no_hi[:, bass.ds(c, 1), :].rearrange("p a t -> p (a t)"), o_ps[:, 0, :], ACT.Copy)\
                  .then_inc(n_hi_done, 1)

            act.wait_ge(set_up, 10)
            with turns(act, NP // 2, A.steps(24) + [(raws[0], 48), (raws[1], 48), (mx, 16), (npv, 4)]) as i:
                for j in range(2):
                    pair(2 * i + j)
            with turns(act, 4, A.steps(2) + [(raws[0], 16), (raws[1], 16)]):
                for _ in range(2):
                    wait_full()
                    split()
            x_final()
            norm(1, 24, PARTS[:1])
            ffn(1, PARTS[:1], True)
            x_final()
            squares(x, KC, LAT)
            root(D, LAT)

        @block.vector
        def _(dve):
            A, B = AccLine(), AccLine()
            hs, slot = Tally(), [0]
            ai, st, sq, hh_t, an, de, vh, qh, ph, pv, gt, gl, ah = (Tally() for _ in range(13))
            ut, sd, tn = [Tally(), Tally()], Tally(), Tally()

            def step(ins):
                ins.then_inc(vec_step, 1)
                dve.wait_ge(vec_step, st.up())

            def split():
                i = slot[0]
                slot[0] = 1 - i
                dve.wait_ge(hi_split, hs.up())
                nc.vector.tensor_tensor(w_lo[i][:, :], raw[i][:, :], w_hi[i][:, :].bitcast(F32), ALU.subtract)\
                  .then_inc(lo_split, 1)

            def wait_full():
                i, full, _, after = A.next()
                dve.wait_ge(acc_full, full)
                return i, acc[i]

            def own_done():
                dve.wait_ge(acc_taken[0], A.taken[0].now())
                dve.wait_ge(acc_taken[1], A.taken[1].now())

            def add_squares(n, width):
                for k in range(n):
                    dve.wait_ge(sq_done, sq.up())
                    if k == 0:
                        ins = nc.vector.tensor_copy(ss[:, 0:width], S[0][:, 0:width])
                    else:
                        dve.wait_ge(sq_added, sq.now() - 1)
                        ins = nc.vector.tensor_tensor(ss[:, 0:width], ss[:, 0:width], S[k % 2][:, 0:width], ALU.add)
                    ins.then_inc(sq_added, 1)

            def one_over(width, on_side=False):
                i, _, _, after = B.next_at(0) if on_side else A.next()
                dve.wait_ge((side_taken if on_side else acc_taken)[i], after)
                step(nc.vector.reciprocal(ss[:, 0:width], ss[:, 0:width]))

            def take_start():
                i, _, _, _ = A.next(counted=False)
                dve.wait_ge(ada_started, 1)
                nc.vector.tensor_tensor(mod[:, 0, 0:16, :], acc[i][:, 0:32].rearrange("p (j c) -> p j c", c=2),
                                        ada_b[:, 0, 0:16].rearrange("p (j c) -> p j c", c=1).to_broadcast([P, 16, 2]),
                                        ALU.add).then_inc(acc_taken[i], 1)

            def ada_step(j, waste, conds=2):
                dve.wait_ge(ada_in, ai.up(16))
                if conds == 2:
                    step(nc.vector.tensor_tensor_reduce(waste[:, 0:D], ada_raw[:, :], silu_rows[:, 1, :], 1.0, 0.0, ALU.mult,
                                                        ALU.add, mod_new[:, j, 1:2]))
                nc.vector.tensor_tensor_reduce(ada_raw[:, :], ada_raw[:, :], silu_rows[:, 0, :], 1.0, 0.0, ALU.mult, ALU.add,
                                               mod_new[:, j, 0:1]).then_inc(ada_used, 1)
                an.up()

            def take_ada(layer, j, n, conds=2):
                dve.wait_ge(ada_used, an.now())
                step(nc.vector.tensor_tensor(mod[:, layer, bass.ds(j, n), 0:conds], mod_new[:, 0:n, 0:conds],
                                             ada_b[:, layer, bass.ds(j, n)].rearrange("p (j c) -> p j c", c=1)
                                             .to_broadcast([P, n, conds]), ALU.add))

            def norm(layer, which, shift, parts, by_column):
                width = TOK if len(parts) > 1 else LAT
                n = len(parts)
                own_done()
                step(nc.vector.scalar_tensor_tensor(
                    norm_a[:, :, 0:n], mod[:, layer, shift + KC:shift + 2 * KC, 0:n], 1.0,
                    norm_w[:, which, :].rearrange("p (k c) -> p k c", c=1).to_broadcast([P, KC, n]), ALU.add, ALU.mult))
                add_squares(KC, width)
                one_over(width)

                def scaled(k):
                    for c0, cn, c in parts:
                        o, a, b = (z[:, c0:c0 + cn] for z in (S[2 + k % 2], x[:, k, :], ss))
                        if by_column and c == 0:
                            o = o.rearrange("p (c r) -> p r c", r=ROWS)
                            a, b = (z.rearrange("p (r c) -> p r c", c=COLS) for z in (a, b))
                        ins = nc.vector.tensor_tensor(o, a, b, ALU.mult)
                    ins.then_inc(norm_t, 1)

                scaled(0)
                for k in range(KC):
                    if k + 1 < KC:
                        scaled(k + 1)
                    dve.wait_ge(norm_t, tn.up())
                    for c0, cn, c in parts:
                        ins = nc.vector.tensor_scalar(S[k % 2][:, c0:c0 + cn], S[2 + k % 2][:, c0:c0 + cn],
                                                      norm_a[:, k, c:c + 1], mod[:, layer, shift + k, c:c + 1],
                                                      ALU.mult, ALU.add)
                    step(ins)
                    dve.wait_ge(h_hi_done, hh_t.up())
                    nc.vector.tensor_tensor(h_lo[:, k, 0:width], S[k % 2][:, 0:width], h_hi[:, k, 0:width].bitcast(F32),
                                            ALU.subtract).then_inc(h_lo_done, 1)

            def add_gated(m, layer, gate, parts):
                i, tile = wait_full()
                for c0, cn, c in parts:
                    xv = x[:, bass.ds(m, 1), c0:c0 + cn].rearrange("p a t -> p (a t)")
                    ins = nc.vector.scalar_tensor_tensor(
                        xv, tile[:, c0:c0 + cn],
                        mod[:, layer, bass.ds(gate + m, 1), c:c + 1].rearrange("p a c -> p (a c)"), xv, ALU.mult, ALU.add)
                ins.then_inc(acc_taken[i], 1)

            def out_projection(with_ada):
                own_done()
                for m in range(KC):
                    add_gated(m, 0, 16, PARTS)
                    if m % 2:
                        split()
                        if m < 2 * with_ada:
                            ada_step(m // 2, S[3])

            def value_lo(vc):
                i, full, _, _ = B.next()
                dve.wait_ge(side_full, full)
                tile = side[i]
                dve.wait_ge(v_hi_done, vh.up())
                hi, lo = (z[:, :].rearrange("p (t v) -> p t v", v=RV)[:, :, vc * P:(vc + 1) * P] for z in (vg_hi, vg_lo))
                nc.vector.tensor_tensor(lo, tile[:, 0:TOK].rearrange("p (t v) -> p t v", v=P), hi.bitcast(F32),
                                        ALU.subtract).then_inc(side_taken[i], 1)

            def rotated(j):
                i, tile = wait_full()
                if j % 2 == 0:
                    table = lambda z, p0, p1: z[p0:p1, :].rearrange("p (r c) -> p r c", c=1).to_broadcast([p1 - p0, ROWS, COLS])
                    cos, sin = cols["cos_r"], cols["sin_r"]
                else:
                    table = lambda z, p0, p1: z[p0:p1, :].rearrange("p (r c) -> p r c", r=1).to_broadcast([p1 - p0, ROWS, COLS])
                    cos, sin = cols["cos_c"], cols["sin_c"]
                grid = lambda z, p0, p1: z[p0:p1, 0:LAT].rearrange("p (r c) -> p r c", c=COLS)
                nc.vector.tensor_tensor(grid(S[0], 0, P), grid(tile, 0, P), table(cos, 0, P), ALU.mult)
                nc.vector.tensor_tensor(grid(S[1], 0, 64), grid(tile, 64, P), table(sin, 64, P), ALU.mult)
                nc.vector.tensor_tensor(grid(S[1], 64, P), grid(tile, 0, 64), table(sin, 0, 64), ALU.mult).then_inc(vec_step, 1)
                split()
                dve.wait_ge(vec_step, st.up())
                nc.vector.tensor_tensor(S[2][:, 0:LAT], S[0][:, 0:LAT], S[1][:, 0:LAT], ALU.add).then_inc(rope_done, 1)
                dve.wait_ge(qk_hi_done, qh.up(2))
                nc.vector.tensor_tensor(qk_lo[:, j, 0:LAT], S[2][:, 0:LAT], qk_hi[:, j, 0:LAT].bitcast(F32), ALU.subtract)
                nc.vector.tensor_tensor(qk_lo[:, j, LAT:TOK], tile[:, LAT:TOK], qk_hi[:, j, LAT:TOK].bitcast(F32),
                                        ALU.subtract).then_inc(acc_taken[i], 1)

            def only_split():
                wait_full()
                split()

            def head_front(hd, first):
                only_split()
                if first:
                    ada_step(0, S[3])
                nc.vector.tensor_copy(head_logs[:, :], logs[:, bass.ds(hd, 1), :].rearrange("p a c -> p (a c)"))
                nc.vector.tensor_scalar(S[0][:, :], dist[:, :], 0.0, None, ALU.max)
                nc.vector.tensor_scalar(S[1][:, :], dist[:, :], -1.0, 0.0, ALU.mult, ALU.max).then_inc(dist_ready, 1)
                only_split()
                dve.wait_ge(decay_exp, de.up(4))
                nc.vector.tensor_tensor(near[:, :], near[:, :], S[1][:, :], ALU.mult)
                step(nc.vector.tensor_tensor(far[:, :], far[:, :], S[0][:, 0:640], ALU.add))
                if first:
                    ada_step(1, S[3])
                    ada_step(2, S[3])
                else:
                    out_projection(3)
                value_lo(0)
                only_split()
                ada_step(3, S[3])
                value_lo(1)
                only_split()
                ada_step(4, S[3])
                value_lo(2)
                rotated(0)
                ada_step(5, S[3])
                value_lo(3)
                for j in range(1, 4):
                    rotated(j)
                    if j < 3:
                        ada_step(5 + j, S[3])
                take_ada(0, hd * 8 + 16, 8)

            def head_attention():
                for i in range(8):
                    _, _, qn, table, c0, _ = SCORES[i]
                    t, tile = wait_full()
                    nc.vector.scalar_tensor_tensor(S[i % 2][:, 0:qn], tile[:, 0:qn], RQK ** -0.5, table[:, c0:c0 + qn],
                                                   ALU.mult, ALU.mult).then_inc(acc_taken[t], 1)
                    dve.wait_ge(p_hi_done, ph.up())
                    nc.vector.tensor_tensor(p_lo[i % 2][:, 0:qn], S[i % 2][:, 0:qn], p_hi[i % 2][:, 0:qn].bitcast(F32),
                                            ALU.subtract).then_inc(p_lo_done, 1)
                add_squares(VC, TOK)

                def gated(g):
                    step(nc.vector.tensor_tensor(vo[:, g, :], vo[:, g, :], ss[:, :], ALU.mult))
                    nc.vector.tensor_tensor(vo[:, g, :], vo[:, g, :], S[2 + g % 2][:, 0:TOK], ALU.mult).then_inc(gate_mul, 1)

                def gated_lo(g):
                    dve.wait_ge(gate_hi, gt.up())
                    nc.vector.tensor_tensor(vg_lo[:, g * TOK:(g + 1) * TOK], vo[:, g, :],
                                            vg_hi[:, g * TOK:(g + 1) * TOK].bitcast(F32), ALU.subtract).then_inc(gate_lo, 1)

                only_split()
                only_split()
                one_over(TOK, on_side=True)
                own_done()
                gated(0)
                gated(1)
                gated_lo(0)
                for g in range(2, 4):
                    i, _, _, after = A.next()
                    dve.wait_ge(acc_full, A.full.now())
                    split()
                    dve.wait_ge(acc_taken[i], after)
                    if g == 2:
                        gated(2)
                        gated_lo(1)
                    else:
                        gated(3)
                gated_lo(2)
                gated_lo(3)

            def ffn(layer, parts, with_ada, ends):
                nj = 0
                width = TOK + 1 if len(parts) > 1 else LAT
                f0 = 0
                for n, size in enumerate(GROUPS):
                    conds = 2 if n == 0 else 1
                    steps = [(hs, 2), (st, 5 + (1 + 2 * (conds - 1) if with_ada else 0)), (ut[0], 1), (ah, 1)]
                    steps += [(ai, 32), (an, 2)] if with_ada else []
                    with turns(dve, size, A.steps(2) + steps) as f:
                        step(nc.vector.tensor_copy(taps[:, :], conv[:, layer, bass.ds(f + f0, 1), :].rearrange("p a c -> p (a c)")))
                        for j in range(2):
                            i, _, _, after = A.next()
                            dve.wait_ge(acc_full, A.full.now())
                            split()
                            dve.wait_ge(acc_taken[i], after)
                            tap = lambda t: taps[:, 4 * j + t:4 * j + t + 1]
                            step(nc.vector.tensor_scalar(S[j][:, 0:width], u[j][:, 0:width], tap(0), tap(3), ALU.mult, ALU.add))
                            step(nc.vector.scalar_tensor_tensor(S[j][:, 0:width], u[j][:, 1:1 + width], tap(1), S[j][:, 0:width],
                                                                ALU.mult, ALU.add))
                            nc.vector.scalar_tensor_tensor(S[j][:, 0:width], u[j][:, 2:2 + width], tap(2), S[j][:, 0:width],
                                                           ALU.mult, ALU.add).then_inc(conv_done, 1)
                            if with_ada and j == 0:
                                ada_step(0, waste, conds)
                        dve.wait_ge(silu_done, ut[0].up())
                        dve.wait_ge(conv_done, ut[0].now() * 2 + (layer + 1))
                        for c0, cn, c in parts:
                            ins = nc.vector.tensor_tensor(S[3][:, c0:c0 + cn], S[2][:, c0 + c:c0 + c + cn],
                                                          S[1][:, c0 + c:c0 + c + cn], ALU.mult)
                        ins.then_inc(act_mul, 1)
                        dve.wait_ge(act_hi_done, ah.up())
                        w = parts[-1][0] + parts[-1][1]
                        hi, lo = (z[:, bass.ds(f, 1), 0:w].rearrange("p a t -> p (a t)") for z in (act_hi, act_lo))
                        nc.vector.tensor_tensor(lo, S[3][:, 0:w], hi.bitcast(F32), ALU.subtract).then_inc(act_lo_done, 1)
                        if with_ada:
                            ada_step(1, waste, conds)
                            take_ada(1, f * 2 + nj, 2, conds)
                    f0 += size
                    nj += 2 * size
                    own_done()
                    pairs = 3 if ends and n == 2 else 4
                    loads = 1 if with_ada and n == 0 else 0
                    with turns(dve, pairs, A.steps(2) + [(hs, 2), (ai, 16 * loads), (an, loads), (st, loads)]) as i:
                        for m in range(2):
                            add_gated(2 * i + m, layer, 40, parts)
                            split()
                        if loads:
                            ada_step(0, waste, 1)
                            take_ada(1, i + nj, 1, 1)
                    nj += 4 * loads
                    if pairs == 3:
                        add_gated(6, layer, 40, parts)
                        add_gated(7, layer, 40, parts)

            def pads():
                for j in range(2):
                    for c in (0, LAT + 1, TOK + 2):
                        ins = nc.vector.memset(u[j][:, c:c + 1], 0.0)
                ins.then_inc(conv_done, 1)

            dve.wait_ge(const_in, 16)
            dve.wait_ge(cond_done, 3)
            step(nc.vector.tensor_scalar(logs[:, :, 0:2], logs[:, :, 0:2], -1.0, None, ALU.mult))
            nc.vector.tensor_scalar(logs[:, :, 2:3], logs[:, :, 0:1], 512.0, None, ALU.mult)
            nc.vector.tensor_scalar(logs[:, :, 3:4], logs[:, :, 1:2], -1.0, None, ALU.mult)
            nc.vector.tensor_scalar(logs[:, :, 4:5], logs[:, :, 1:2], 256.0, None, ALU.mult)
            step(nc.vector.memset(logs[:, :, 5:8], 0.0))
            for _ in range(2):
                split()
            take_start()
            dve.wait_ge(x_loaded, 16)
            dve.wait_ge(set_up, 2)
            norm(0, 0, 0, PARTS, False)
            head_front(0, True)
            head_attention()
            with turns(dve, RH - 1, A.steps(HEAD_TILES + 8) + B.steps(HEAD_SIDE, 1) + [(ai, 128), (hs, 16), (st, 19), (sq, VC), (an, 8), (de, 4), (vh, 4),
                                                                 (qh, 8), (ph, 8), (gt, 4)]) as hd:
                head_front(hd + 1, False)
                head_attention()
            out_projection(0)
            pads()
            norm(0, 2, 24, PARTS, False)
            ffn(0, PARTS, True, False)
            norm(1, 1, 0, PARTS, True)
            nh, sf, ex, pd, pth, bd = (Tally() for _ in range(6))

            def maximum(i):
                hh, a = divmod(i, QB)
                n = WIN[a][1] * ROWS + CTX
                dve.wait_ge(s_full, sf.up())
                nc.vector.memset(top[:, i % 2, 5:6], 0.0)
                nc.vector.tensor_tensor_reduce(S[i % 2][:, 0:n], o_ps[:, 1 + i % 2, 0:n], bias[hh][:, MASKS[a], 0:n], 1.0, -3e38,
                                               ALU.add, ALU.max, top[:, i % 2, 0:1]).then_inc(s_taken, 1)
                dve.wait_ge(s_taken, sf.now() + 1)
                nc.vector.tensor_scalar(top[:, i % 2, 1:2], top[:, i % 2, 0:1], -1.0, None, ALU.mult).then_inc(max_done, 1)

            def one_over_sum(i):
                dve.wait_ge(exp_done, ex.up())
                step(nc.vector.tensor_tensor(top[:, i % 2, 4:5], top[:, i % 2, 2:3], top[:, i % 2, 3:4], ALU.add))
                nc.vector.reciprocal(top[:, i % 2, 4:5], top[:, i % 2, 4:5]).then_inc(sum_done, 1)

            def probs_lo(i):
                a = i % QB
                t, tile = wait_full()
                dve.wait_ge(pt_hi_done, pth.up())
                t0, tn = TILES[a]
                for z0, zn, c0 in ((t0, tn, 0), (4, 2, tn * P)):
                    hi, lo = (z[:, z0:z0 + zn, a * P:(a + 1) * P] for z in (pt_hi, pt_lo))
                    ins = nc.vector.tensor_tensor(lo, tile[:, c0:c0 + zn * P].rearrange("p (t q) -> p t q", q=P),
                                                  hi.bitcast(F32), ALU.subtract)
                ins.then_inc(acc_taken[t], 1)

            def pair(c):
                t, tile = wait_full()
                dve.wait_ge(n_hi_done, nh.up(2))
                for hh in range(2):
                    ins = nc.vector.scalar_tensor_tensor(nq[ND:P, hh, :], tile[hh * ND:(hh + 1) * ND, 0:LAT], ND ** -0.5,
                                                         nq[0:ND, hh, :].bitcast(F32), ALU.mult, ALU.subtract)
                ins.then_inc(acc_taken[t], 1)
                split()
                t, tile = wait_full()
                dve.wait_ge(n_hi_done, nh.up(4))
                for hh in range(2):
                    for half in range(2):
                        own = slice(half * ND, (half + 1) * ND)
                        ins = nc.vector.tensor_tensor(nk_lo[own, hh, :], tile[hh * ND:(hh + 1) * ND, 0:TOK],
                                                      nk_hi[own, hh, :].bitcast(F32), ALU.subtract)
                ins.then_inc(acc_taken[t], 1)
                split()
                only_split()
                t, tile = wait_full()
                dve.wait_ge(n_hi_done, nh.up(2))
                for hh in range(2):
                    own = slice(hh * ND, (hh + 1) * ND)
                    ins = nc.vector.tensor_tensor(nv_lo[:, :, hh, own], tile[:, 0:TOK].rearrange("p (t v) -> p t v", v=P)[:, :, own],
                                                  nv_hi[:, :, hh, own].bitcast(F32), ALU.subtract)
                ins.then_inc(acc_taken[t], 1)
                dve.wait_ge(bias_done, bd.up(6))
                maximum(0)
                maximum(1)
                one_over_sum(0)
                for i in range(8):
                    if i + 2 < 8:
                        maximum(i + 2)
                    if i + 1 < 8:
                        one_over_sum(i + 1)
                    probs_lo(i)
                dve.wait_ge(n_hi_done, nh.up(1))
                hi, lo = (z[:, bass.ds(c, 1), :].rearrange("p a t -> p (a t)") for z in (no_hi, no_lo))
                nc.vector.tensor_tensor(lo, o_ps[:, 0, :], hi.bitcast(F32), ALU.subtract).then_inc(no_taken, 1)

            nc.vector.memset(top[:, 0, 5:6], 0.0).then_inc(s_taken, 1)
            nc.vector.memset(top[:, 1, 5:6], 0.0).then_inc(no_taken, 1)
            dve.wait_ge(set_up, 10)
            with turns(dve, NP // 2, A.steps(24) + [(hs, 6), (st, 16), (nh, 18), (sf, 16), (ex, 16), (pth, 16), (bd, 12)]) as i:
                for j in range(2):
                    pair(2 * i + j)
            dve.wait_ge(x_back, 16)
            with turns(dve, 4, A.steps(2) + [(hs, 2)]) as i:
                for m in range(2):
                    t, tile = wait_full()
                    xv = x[:, bass.ds(2 * i + m, 1), 0:LAT].rearrange("p a (r c) -> p c (a r)", c=COLS)
                    nc.vector.scalar_tensor_tensor(
                        xv, tile[:, 0:LAT].rearrange("p (c r) -> p c r", r=ROWS),
                        mod[:, 1, bass.ds(2 * i + (16 + m), 1), 0:1].rearrange("p a c -> p (a c)"), xv,
                        ALU.mult, ALU.add).then_inc(acc_taken[t], 1)
                    split()
            pads()
            norm(1, 3, 24, PARTS[:1], False)
            ffn(1, PARTS[:1], False, True)
            own_done()
            add_squares(KC, LAT)
            one_over(LAT)
            for k in range(KC):
                step(nc.vector.tensor_tensor(x[:, k, 0:LAT], x[:, k, 0:LAT], ss[:, 0:LAT], ALU.mult))
                nc.vector.tensor_scalar(x[:, k, 0:LAT], x[:, k, 0:LAT], norm_w[:, 4, k:k + 1], None, ALU.mult)\
                  .then_inc(x_ready, 1)


def tiled(w):
    *lead, k, m = w.shape
    n = len(lead)
    w = w.reshape(*lead, k // P, P, m // P, P)
    return w.transpose(*range(n), n + 2, n + 1, n, n + 3)


def weight_stream(w_in, r_out, w_qkv, n_out, up, down):
    chunks = []
    put = lambda c: chunks.append(np.ascontiguousarray(c).reshape(P, D))
    win = tiled(w_in)
    ro = tiled(r_out.reshape(RH, RV, D))
    qk, v, g = RH * 2, RH * 4, RH * 8

    def put_out(h):
        for s in range(OUT_SLOTS):
            put(ro[h, 2 * s:2 * s + 2].transpose(1, 0, 2, 3))

    def put_ffn(layer):
        u = tiled(up[layer])
        f0 = 0
        for size in GROUPS:
            for f in range(f0, f0 + size):
                put(u[f])
                put(u[FC + f])
            dn = tiled(down[layer][f0 * P:(f0 + size) * P])
            for m in range(KC):
                put(np.pad(dn[m], ((0, 0), (0, 8 - size), (0, 0))))
            f0 += size

    for h in range(RH):
        put(win[2 * qk + 4 * h])
        put(win[2 * qk + 4 * h + 1])
        if h:
            put_out(h - 1)
        put(win[2 * qk + 4 * h + 2])
        put(win[2 * qk + 4 * h + 3])
        for j in range(2):
            put(win[qk + 2 * h + j])
        for j in range(2):
            put(win[2 * h + j])
        for j in range(4):
            put(win[2 * qk + RH * 4 + 4 * h + j])
    put_out(RH - 1)
    put_ffn(0)
    qkv = tiled(w_qkv)
    for c in range(NP):
        for j in range(3):
            put(qkv[j * KC + c])
    no = tiled(n_out)
    for m in range(KC):
        put(no[m])
    put_ffn(1)
    assert len(chunks) == CHUNKS
    return np.stack(chunks)


def by_feature(a):
    a = a.reshape(*a.shape[:-1], KC, P)
    return np.moveaxis(a, -1, 0)


def rope_tables():
    q = RQK // 4
    inv = np.float32(10000.0) ** (-np.arange(q, dtype=np.float32) / np.float32(q))
    inv = np.concatenate([inv, inv])[:, None].astype(np.float32)
    sign = np.where(np.arange(P) < q, 1, -1)[:, None].astype(np.float32)
    out = []
    for n in (ROWS, COLS):
        ang = np.arange(n, dtype=np.float32)[None, :] * inv
        out += [np.cos(ang).astype(np.float32), (np.sin(ang) * sign).astype(np.float32)]
    return out


def mask_tables():
    c = np.arange(16)[:, None]
    k = np.arange(32)[None, :]
    out = []
    for first in (0, 16, 48):
        query, key = c + first, k + first - 8
        start = np.clip(query - NKW // 2, 0, COLS - NKW)
        ok = (key >= start) & (key < start + NKW)
        m = np.where(ok, 0.0, -1e30).astype(np.float32)
        out.append(np.broadcast_to(m[:, None, :, None], (16, ROWS, 32, ROWS)).reshape(P, 256))
    return np.ascontiguousarray(np.stack(out, 1))


def relative(rpb):
    padded = np.pad(rpb, ((0, 0), (0, 0), (8, 8)))
    c, r = np.divmod(np.arange(P), ROWS)
    k, kr = np.divmod(np.arange(256), ROWS)
    dr = kr[None, :] - r[:, None] + ROWS - 1
    dc = k[None, :] - c[:, None] + 7 + 8
    return np.ascontiguousarray(padded[:, dr, dc])


def kernel(**inputs):
    import concourse.bacc as bacc
    from concourse.bass_utils import run_bass_kernel_spmd

    a = {k: np.asarray(v) for k, v in inputs.items()}
    tokens = np.concatenate([a["x"][0], a["ctx"][0]])
    x_in = np.ascontiguousarray(by_feature(tokens).transpose(0, 2, 1))
    weights = weight_stream(a["ret_w_in"][0], a["ret_w_out"][0], a["na_w_qkv"][0], a["na_w_out"][0],
                            a["ffn_w_up"], a["ffn_w_down"])
    ada_first = np.ascontiguousarray(tiled(a["ada_w"][0, :, :16 * P])).reshape(16, P, D)
    ada = np.ascontiguousarray(a["ada_w"].transpose(0, 2, 1)).reshape(96, P, D)[16:]
    norm_w = np.stack([a["norm1_w"][0], a["norm1_w"][1], a["norm2_w"][0], a["norm2_w"][1], a["final_norm_w"]])
    taps = np.concatenate([a["ffn_conv_w"], a["ffn_conv_b"][:, None]], 1)
    taps = taps.reshape(2, 4, 2, FC, P).transpose(4, 0, 3, 2, 1)
    cos_r, sin_r, cos_c, sin_c = rope_tables()
    parts = {
        "cond": by_feature(np.stack([a["c"][0], a["c_ctx"]])).transpose(0, 2, 1),
        "norm_w": by_feature(norm_w),
        "ada_b": a["ada_b"].reshape(2, 48, P).transpose(2, 0, 1),
        "dlog": np.broadcast_to(np.stack([a["ret_decay_fwd"][0], a["ret_decay_bwd"][0]], 1)[None], (P, RH, 2)),
        "cos_r": cos_r, "sin_r": sin_r, "cos_c": cos_c, "sin_c": sin_c,
        "conv": taps, "ident": np.eye(P, dtype=np.float32),
    }
    small = np.concatenate([np.ascontiguousarray(parts[n]).reshape(P, -1) for n, _ in SMALL], 1)
    arrays = {"x_in": x_in, "weights": weights, "ada_first": ada_first, "ada": np.ascontiguousarray(ada),
              "cond_rows": np.stack([a["c"][0], a["c_ctx"]]), "small": np.ascontiguousarray(small),
              "bias": relative(a["na_rpb"][0]), "masks": mask_tables()}
    nc = bacc.Bacc("TRN2", target_bir_lowering=False, num_devices=1)
    aps = [nc.dram_tensor(f"in_{n}_dram", v.shape, F32, kind="ExternalInput").ap() for n, v in arrays.items()]
    park = nc.dram_tensor("park_dram", (P, KC, LAT), F32, kind="Internal").ap()
    out = nc.dram_tensor("out_dram", (P, KC, LAT), F32, kind="ExternalOutput").ap()
    backbone(nc, *aps, park, out)
    r = run_bass_kernel_spmd(nc, [{f"in_{n}_dram": v for n, v in arrays.items()}], core_ids=[0])
    y = r.results[0]["out_dram"]
    return np.ascontiguousarray(y.transpose(2, 1, 0)).reshape(1, LAT, D)
```

```python
from contextlib import ExitStack, contextmanager

import numpy as np
import concourse.bass as bass
from concourse import mybir

F32 = mybir.dt.float32
F32R = mybir.dt.float32r
ALU = mybir.AluOpType
ACT = mybir.ActivationFunctionType

P = 128
D = 1024
KC = D // P
LAT, CTX = 512, 256
TOK = LAT + CTX
ROWS, COLS = LAT // 64, 64
EPS = 1e-6
RH, RQK, RV = 4, 256, 512
VC = RV // P
TT = TOK // P
NH, ND, NKW = 16, 64, 16
NP = NH // 2
QB = 4
F = 2816
FC = F // P
GROUPS = (8, 8, 6)
UP_ADA, DOWN_ADA = (1, 1, 0), (3, 3, 2)
OUT_SLOTS = 4
CHUNKS = RH * (12 + OUT_SLOTS) + 2 * (2 * FC + 8 * len(GROUPS)) + 3 * NP + 8
PARTS = ((0, LAT, 0), (LAT, CTX, 1))
WIN = ((0, 24), (8, 32), (24, 32), (40, 24))
TILES = ((0, 2), (0, 3), (1, 3), (2, 2))
MASKS = (0, 1, 1, 2)
SMALL = (("cond", 16), ("norm_w", 40), ("ada_b", 96), ("dlog", 8), ("cos_r", 8), ("sin_r", 8),
         ("cos_c", 64), ("sin_c", 64), ("conv", 2 * FC * 8), ("ident", P))
NSMALL = sum(n for _, n in SMALL)


class Tally:

    def __init__(self):
        self.base, self.n = 0, 0

    def now(self):
        return self.base + self.n if self.n else self.base

    def up(self, k=1):
        self.n += k
        return self.now()

    def began(self):
        return not (isinstance(self.base, int) and self.base + self.n == 0)


@contextmanager
def turns(eng, trips, steps):
    was = [(t, t.base, t.n) for t, _ in steps]
    with eng.Fori(0, trips) as i:
        for t, k in steps:
            t.base, t.n = eng.snap(i * k + t.now()), 0
        yield i
        left = [(j, t.n, k) for j, (t, k) in enumerate(steps) if t.n != k]
        assert not left, f"tallies (index, made, promised): {left}"
    for (t, base, n), (_, k) in zip(was, steps):
        t.base, t.n = base, n + trips * k


class AccLine:

    def __init__(self):
        self.full, self.taken, self.turn = Tally(), (Tally(), Tally()), 0

    def next(self, counted=True):
        i = self.turn
        self.turn = 1 - i
        full = self.full.up() if counted else None
        began = self.taken[i].began()
        before = self.taken[i].now()
        return i, full, (before if began else None), self.taken[i].up()

    def next_at(self, i):
        turn, self.turn = self.turn, i
        got = self.next()
        self.turn = turn
        return got

    def steps_at(self, tiles0, tiles1):
        return [(self.full, tiles0 + tiles1), (self.taken[0], tiles0), (self.taken[1], tiles1)]

    def steps(self, tiles, extra0=0):
        assert tiles % 2 == 0
        return [(self.full, tiles + extra0), (self.taken[0], tiles // 2 + extra0), (self.taken[1], tiles // 2)]


def backbone(nc, x_in, weights, ada_first, ada, cond_rows, small_in, bias_in, masks_in, park, out):
    ctx = ExitStack()
    with ctx:
        def sem(name):
            return ctx.enter_context(nc.semaphore(name))

        def sb(name, shape, dt=F32, stack=ctx):
            return stack.enter_context(nc.sbuf_tensor(name, shape, dt))

        with ExitStack() as part:
            x = sb("x", [P, KC, TOK], stack=part)
        pt_hi = sb("pt_hi", [P, TT, QB * P], F32R)
        pt_lo = sb("pt_lo", [P, TT, QB * P], F32R)
        h_hi = sb("h_hi", [P, KC, TOK], F32R)
        h_lo = sb("h_lo", [P, KC, TOK], F32R)
        raw = [sb(f"raw{i}", [P, D]) for i in range(2)]
        w_hi = [sb(f"w_hi{i}", [P, D], F32R) for i in range(2)]
        w_lo = [sb(f"w_lo{i}", [P, D], F32R) for i in range(2)]
        small = sb("small", [P, NSMALL])
        mod = sb("mod", [P, 2, 48, 2])
        norm_a = sb("norm_a", [P, KC, 2])
        silu_c = sb("silu_c", [P, KC, 2])
        nothing = sb("nothing", [P, 1])
        ones = sb("ones", [P, P])
        ss = sb("ss", [P, TOK])
        S = [sb(f"scratch{i}", [P, 1024 if i == 3 else 896]) for i in range(4)]
        mod_new = sb("mod_new", [P, 8, 2])
        at, cols = 0, {}
        for name, n in SMALL:
            cols[name] = small[:, at:at + n]
            at += n
        cond = cols["cond"].rearrange("p (k c) -> p k c", c=2)
        norm_w = cols["norm_w"].rearrange("p (n k) -> p n k", k=KC)
        ada_b = cols["ada_b"].rearrange("p (l j) -> p l j", l=2)
        conv = cols["conv"].rearrange("p (l f c) -> p l f c", l=2, c=8)
        ident = cols["ident"]

        with ExitStack() as stage:
            ada_raw = sb("ada_raw", [P, D], stack=stage)
            silu_rows = sb("silu_rows", [P, 2, D], stack=stage)
            with ExitStack() as part:
                ada_start = [sb(f"ada_start{i}", [P, 4, D], stack=part) for i in range(4)]
            with ExitStack() as part:
                qk_hi = sb("qk_hi", [P, 4, TOK], F32R, part)
                qk_lo = sb("qk_lo", [P, 4, TOK], F32R, part)
                vg_hi = sb("vg_hi", [P, VC * TOK], F32R, part)
                vg_lo = sb("vg_lo", [P, VC * TOK], F32R, part)
                vo = sb("vo", [P, VC, TOK], stack=part)
                p_hi = [sb(f"p_hi{i}", [P, LAT], F32R, part) for i in range(2)]
                p_lo = [sb(f"p_lo{i}", [P, LAT], F32R, part) for i in range(2)]
                dist = sb("dist", [P, 896], stack=part)
                near = sb("near", [P, 896], stack=part)
                far = sb("far", [P, 640], stack=part)
                logs = sb("logs", [P, RH, 8], stack=part)
                head_logs = sb("head_logs", [P, 8], stack=part)
            with ExitStack() as part:
                act_hi = sb("act_hi", [P, 8, TOK], F32R, part)
                act_lo = sb("act_lo", [P, 8, TOK], F32R, part)
                u = [sb(f"u{i}", [P, TOK + 4], stack=part) for i in range(2)]
                taps = sb("taps", [P, 8], stack=part)
                waste = sb("waste", [P, D], stack=part)
        with ExitStack() as stage:
            masks = sb("masks", [P, 3, 256], stack=stage)
            rel = [sb(f"rel{i}", [P, 256], stack=stage) for i in range(2)]
            nq = sb("nq", [P, 2, LAT], F32R, stage)
            nk_hi = sb("nk_hi", [P, 2, TOK], F32R, stage)
            nk_lo = sb("nk_lo", [P, 2, TOK], F32R, stage)
            nv_hi = sb("nv_hi", [P, TT, 2, P], F32R, stage)
            nv_lo = sb("nv_lo", [P, TT, 2, P], F32R, stage)
            prob = [sb(f"prob{a}", [P, TILES[a][1] * P + CTX], stack=stage) for a in range(QB)]
            bias = [sb(f"bias{i}", [P, 3, LAT], stack=stage) for i in range(2)]
            no_hi = sb("no_hi", [P, NP, LAT], F32R, stage)
            no_lo = sb("no_lo", [P, NP, LAT], F32R, stage)
            top = sb("top", [P, 2, 8], stack=stage)

        acc = [ctx.enter_context(nc.psum_tensor(f"acc{i}", [P, 2 * LAT], F32)) for i in range(2)]
        o_ps = ctx.enter_context(nc.psum_tensor("o_ps", [P, VC, LAT], F32))
        side = [o_ps[:, 2 * i:2 * i + 2, :].rearrange("p a t -> p (a t)") for i in range(2)]

        acc_full = sem("acc_full")
        acc_taken = [sem("acc_taken0"), sem("acc_taken1")]
        const_in, x_loaded, masks_loaded = sem("const_in"), sem("x_loaded"), sem("masks_loaded")
        raw_in = [sem("raw_in0"), sem("raw_in1")]
        hi_split, lo_split = sem("hi_split"), sem("lo_split")
        ada_start_in = [sem(f"ada_start_in{i}") for i in range(4)]
        rows_in, ada_in, ada_used, ada_started = sem("rows_in"), sem("ada_in"), sem("ada_used"), sem("ada_started")
        side_full, side_taken = sem("side_full"), [sem("side_taken0"), sem("side_taken1")]
        set_up = sem("set_up")
        cond_done = sem("cond_done")
        vec_step = sem("vec_step")
        sq_done, sq_added = sem("sq_done"), sem("sq_added")
        norm_t, h_hi_done, h_lo_done = sem("norm_t"), sem("h_hi_done"), sem("h_lo_done")
        dist_ready, decay_exp = sem("dist_ready"), sem("decay_exp")
        v_hi_done = sem("v_hi_done")
        rope_done, qk_hi_done = sem("rope_done"), sem("qk_hi_done")
        p_hi_done, p_lo_done, pv_done, o_taken = sem("p_hi_done"), sem("p_lo_done"), sem("pv_done"), sem("o_taken")
        gate_mul, gate_hi, gate_lo = sem("gate_mul"), sem("gate_hi"), sem("gate_lo")
        conv_done, silu_done, act_mul = sem("conv_done"), sem("silu_done"), sem("act_mul")
        act_hi_done, act_lo_done = sem("act_hi_done"), sem("act_lo_done")
        rel_in, bias_done, parked, x_back = sem("rel_in"), sem("bias_done"), sem("parked"), sem("x_back")
        n_hi_done = sem("n_hi_done")
        s_full, s_taken, max_done, exp_done = sem("s_full"), sem("s_taken"), sem("max_done"), sem("exp_done")
        prob_done, pt_hi_done = sem("prob_done"), sem("pt_hi_done")
        npv_done, no_taken = sem("npv_done"), sem("no_taken")
        q_full, q_taken = sem("q_full"), sem("q_taken")
        x_ready, x_out = sem("x_ready"), sem("x_out")

        SCORES = [(LAT + P * j, LAT, CTX, near, 384 - P * j, 4 + j) for j in range(2)]
        SCORES += [(P * j, 0, LAT, near, 384 - P * j, j) for j in range(4)]
        SCORES += [(LAT + P * j, 0, LAT, far, P - P * j, 4 + j) for j in range(2)]
        HEAD_CHUNKS = 12
        HEAD_TILES = 4 + 4 + 8 + 4
        HEAD_SIDE = 4

        block = ctx.enter_context(nc.Block())

        @block.sync
        def _(sp):
            sp.dma_start(small[:, :], small_in).then_inc(const_in, 16)
            for c in range(2):
                sp.dma_start(silu_rows[:, c, :], cond_rows[c, :].partition_broadcast(P)).then_inc(rows_in, 16)
            for i in (2, 0, 1, 3):
                if i == 1:
                    sp.dma_start(x[:, :, :], x_in).then_inc(x_loaded, 16)
                sp.dma_start(ada_start[i][:, :, :], ada_first[4 * i:4 * i + 4, :, :].rearrange("a p n -> p a n"))\
                  .then_inc(ada_start_in[i], 16)
            sp.dma_start(raw[0][:, :], weights[0, :, :]).then_inc(raw_in[0], 16)
            sp.dma_start(raw[1][:, :], weights[1, :, :]).then_inc(raw_in[1], 16)
            with sp.Fori(1, CHUNKS // 2) as i:
                for slot in range(2):
                    sp.wait_ge(lo_split, i * 2 + (slot - 1))
                    sp.dma_start(raw[slot][:, :], weights[bass.ds(i * 2 + slot, 1), :, :].rearrange("a p n -> p (a n)"))\
                      .then_inc(raw_in[slot], 16)
            for k in range(KC):
                sp.wait_ge(x_ready, k + 1)
                sp.dma_start(out[:, k, :], x[:, k, 0:LAT]).then_inc(x_out, 16)
            sp.wait_ge(x_out, 16 * KC)

        @block.gpsimd
        def _(pool):
            pool.dma_start(ada_raw[:, :], ada[0, :, :]).then_inc(ada_in, 16)
            nc.gpsimd.memset(ones[:, :], 1.0).then_inc(set_up, 1)
            nc.gpsimd.iota(dist[:, :], pattern=[[1, 896]], base=-384, channel_multiplier=-1,
                           allow_small_or_imprecise_dtypes=True).then_inc(set_up, 1)
            with pool.Fori(1, 80) as i:
                pool.wait_ge(ada_used, i)
                pool.dma_start(ada_raw[:, :], ada[bass.ds(i, 1), :, :].rearrange("a p n -> p (a n)")).then_inc(ada_in, 16)

            pool.wait_ge(norm_t, 2 * KC + 1)
            pool.dma_start(masks[:, :, :], masks_in).then_inc(masks_loaded, 16)
            zeros = [nv_hi[:, :, :, :].bitcast(F32), nv_lo[:, :, :, :].bitcast(F32)] + [prob[a][:, :] for a in range(QB)]
            zeros += [bias[i][:, :, :] for i in range(2)]
            for z in zeros:
                nc.gpsimd.memset(z, 0.0).then_inc(set_up, 1)
            pool.wait_ge(norm_t, 3 * KC)
            pool.dma_start(park, x[:, :, 0:LAT]).then_inc(parked, 16)

            rels, biases, taken = Tally(), Tally(), Tally()

            def load_rel(c, hh):
                pool.dma_start(rel[hh][:, :], bias_in[bass.ds(c * 2 + hh, 1), :, :].rearrange("a p n -> p (a n)"))\
                    .then_inc(rel_in, 16)

            def make_bias(hh):
                for m, (lo, n) in enumerate(((64, 192), (0, 256), (0, 192))):
                    nc.gpsimd.tensor_tensor(bias[hh][:, m, 0:n], rel[hh][:, lo:lo + n], masks[:, m, lo:lo + n], ALU.add)\
                        .then_inc(bias_done, 1)
                biases.up(3)

            load_rel(0, 0)
            load_rel(0, 1)
            pool.wait_ge(masks_loaded, 16)
            pool.wait_ge(set_up, 2 + len(zeros))
            pool.wait_ge(rel_in, rels.up(32))
            make_bias(0)
            make_bias(1)
            with turns(pool, NP - 1, [(rels, 32), (biases, 6), (taken, 8)]) as c:
                pool.wait_ge(bias_done, biases.now())
                load_rel(c + 1, 0)
                load_rel(c + 1, 1)
                pool.wait_ge(rel_in, rels.up(32))
                for hh in range(2):
                    pool.wait_ge(s_taken, taken.up(4) + 1)
                    make_bias(hh)
            pool.wait_ge(npv_done, 2 * NP)
            pool.wait_ge(parked, 16)
            pool.dma_start(x[:, :, 0:LAT], park).then_inc(x_back, 16)

        @block.tensor
        def _(pe):
            A, B = AccLine(), AccLine()
            chunk = Tally()
            squares_added, h_split, p_split, o_left, gates_split, act_split = Tally(), Tally(), Tally(), Tally(), Tally(), Tally()
            slot, opened, value_tiles = [0], [None], {}

            def open_acc(counted=True):
                i, _, before, after = A.next(counted)
                if before is not None:
                    pe.wait_ge(acc_taken[i], before)
                opened[0] = (i, after)
                return acc[i]

            def open_side(got):
                i, _, before, after = got
                if before is not None:
                    pe.wait_ge(side_taken[i], before)
                return side[i]

            def next_chunk():
                pe.wait_ge(lo_split, chunk.up())
                i = slot[0]
                slot[0] = 1 - i
                return w_hi[i], w_lo[i]

            def product(tile, w, blocks, hi, lo, parts, ready=None):
                last = len(blocks) - 1
                for n, b in enumerate(blocks):
                    if ready is not None:
                        ready(n)
                    for m, (wt, mv) in enumerate(((w[0], hi), (w[0], lo), (w[1], hi))):
                        for c0, cn, _ in parts:
                            mm = nc.tensor.matmul(tile[:, c0:c0 + cn], wt[:, b * P:(b + 1) * P], mv[:, n, c0:c0 + cn],
                                                  start=(n == 0 and m == 0), stop=(n == last and m == 2))
                mm.then_inc(acc_full, 1)

            def project(hi, lo, parts, ready=None):
                w = next_chunk()
                product(open_acc(), w, range(KC), hi, lo, parts, ready)

            def start_ada():
                tile = open_acc(counted=False)
                for i in range(2):
                    if i == 1:
                        pe.wait_ge(set_up, 1)
                        ones_tile(KC, PARTS)
                    pe.wait_ge(ada_start_in[i], 16)
                    for j in range(4):
                        at = 2 * (4 * i + j)
                        for k in range(KC):
                            mm = nc.tensor.matmul(tile[:, at:at + 2], ada_start[i][:, j, k * P:(k + 1) * P],
                                                  silu_c[:, k, :], start=(k == 0), stop=(k == KC - 1))
                mm.then_inc(ada_started, 1)

            def ones_tile(n, parts, on_side=False):
                pe.wait_ge(sq_added, squares_added.up(n))
                tile = open_side(B.next_at(0)) if on_side else open_acc()
                for c0, cn, _ in parts:
                    mm = nc.tensor.matmul(tile[:, c0:c0 + cn], ones[:, :], ss[:, c0:c0 + cn], start=True, stop=True)
                mm.then_inc(side_full if on_side else acc_full, 1)

            def h_ready(first):
                return lambda n: pe.wait_ge(h_lo_done, first + n + 1)

            def head_front(hd, first):
                ready = None
                if first:
                    ready = h_ready(h_split.now())
                    h_split.up(KC)
                project(h_hi, h_lo, PARTS, ready)
                value_tiles[0] = opened[0]
                project(h_hi, h_lo, PARTS)
                value_tiles[1] = opened[0]
                if not first:
                    out_projection()
                turn_values(0)
                project(h_hi, h_lo, PARTS)
                value_tiles[2] = opened[0]
                turn_values(1)
                project(h_hi, h_lo, PARTS)
                value_tiles[3] = opened[0]
                turn_values(2)
                project(h_hi, h_lo, PARTS)
                turn_values(3)
                for _ in range(3):
                    project(h_hi, h_lo, PARTS)

            def turn_values(vc):
                i, after = value_tiles[vc]
                pe.wait_ge(acc_taken[i], after)
                tile = open_side(B.next())
                for t in range(TT):
                    mm = nc.tensor.transpose(tile[:, t * P:(t + 1) * P], vo[:, vc, t * P:(t + 1) * P], ident)
                mm.then_inc(side_full, 1)

            def scores(i):
                k0, q0, qn, _, _, _ = SCORES[i]
                tile = open_acc()
                for d in range(2):
                    for m, (kt, q_left) in enumerate(((qk_hi, qk_hi), (qk_hi, qk_lo), (qk_lo, qk_hi))):
                        mm = nc.tensor.matmul(tile[:, 0:qn], kt[:, d, k0:k0 + P], q_left[:, 2 + d, q0:q0 + qn],
                                              start=(d == 0 and m == 0), stop=(d == 1 and m == 2))
                mm.then_inc(acc_full, 1)

            def values(tiles, first, last):
                for vc in range(VC):
                    for n, i in enumerate(tiles):
                        _, _, qn, _, _, t = SCORES[i]
                        c0 = t * RV + vc * P
                        for m, (vt, pt) in enumerate(((vg_hi, p_hi), (vg_hi, p_lo), (vg_lo, p_hi))):
                            mm = nc.tensor.matmul(o_ps[:, vc, 0:qn], vt[:, c0:c0 + P], pt[i % 2][:, 0:qn],
                                                  start=(first and n == 0 and m == 0),
                                                  stop=(last and n == len(tiles) - 1 and m == 2))
                mm.then_inc(pv_done, 1)

            def head_attention():
                split_done = [A.taken[i].now() for i in range(2)]
                project(h_hi, h_lo, PARTS)
                for i in range(2):
                    pe.wait_ge(acc_taken[i], split_done[i])
                scores(0)
                scores(1)
                scores(2)
                pe.wait_ge(p_lo_done, p_split.up(2))
                for i in range(2):
                    pe.wait_ge(side_taken[i], B.taken[i].now())
                values((0, 1), True, True)
                pe.wait_ge(o_taken, o_left.up())
                for i in range(2, 8):
                    if i < 7:
                        scores(i + 1)
                    pe.wait_ge(p_lo_done, p_split.up())
                    values((i,), i == 2, i == 7)
                o_left.up()
                project(h_hi, h_lo, PARTS)
                ones_tile(VC, PARTS, on_side=True)
                project(h_hi, h_lo, PARTS)
                project(h_hi, h_lo, PARTS)

            def out_projection():
                pe.wait_ge(gate_lo, gates_split.up(VC))
                hi = vg_hi[:, :].rearrange("p (k t) -> p k t", k=VC)
                lo = vg_lo[:, :].rearrange("p (k t) -> p k t", k=VC)
                for _ in range(OUT_SLOTS):
                    w = next_chunk()
                    for m in range(2):
                        product(open_acc(), w, range(m * VC, (m + 1) * VC), hi, lo, PARTS)

            def ffn(parts):
                ready = h_ready(h_split.now())
                first = True
                for size in GROUPS:
                    at = act_split.now()

                    def act_ready(n):
                        pe.wait_ge(act_lo_done, at + n + 1)

                    if first:
                        h_split.up(KC)
                    with turns(pe, size, A.steps(2) + [(chunk, 2)]):
                        project(h_hi, h_lo, parts, ready if first else None)
                        project(h_hi, h_lo, parts)
                    first = False
                    act_split.up(size)
                    with turns(pe, 4, A.steps(2) + [(chunk, 2)]):
                        for m in range(2):
                            w = next_chunk()
                            product(open_acc(), w, range(size), act_hi, act_lo, parts, act_ready if m == 0 else None)

            s_left, probs_ready, pairs_done, q_left = Tally(), Tally(), Tally(), Tally()

            def block_scores(i):
                hh, a = divmod(i, QB)
                pe.wait_ge(s_taken, s_left.now() + max(i, 1))
                tile = o_ps[:, 1 + i % 2, :]
                q = nq[:, hh, a * P:(a + 1) * P]
                w0, wn = WIN[a][0] * ROWS, WIN[a][1] * ROWS
                for c0, k0, n in ((0, w0, wn), (wn, LAT, CTX)):
                    for m, nk in enumerate((nk_hi, nk_lo)):
                        mm = nc.tensor.matmul(tile[:, c0:c0 + n], q, nk[:, hh, k0:k0 + n], start=(m == 0), stop=(m == 1))
                mm.then_inc(s_full, 1)

            def turn_probs(i):
                a = i % QB
                pe.wait_ge(prob_done, probs_ready.up())
                tile = open_at(0)
                for t in range(TILES[a][1] + 2):
                    mm = nc.tensor.transpose(tile[:, t * P:(t + 1) * P], prob[a][:, t * P:(t + 1) * P], ident)
                mm.then_inc(acc_full, 1)

            def pair_values(hh):
                pe.wait_ge(acc_taken[0], A.taken[0].now())
                if hh == 0:
                    pe.wait_ge(no_taken, pairs_done.now() + 1)
                for n, t in enumerate((4, 5, 0, 1, 2, 3)):
                    a0, a1 = (0, QB) if t >= 4 else (max(0, t - 1), min(QB, t + 2))
                    for m, (vt, pt) in enumerate(((nv_hi, pt_hi), (nv_hi, pt_lo), (nv_lo, pt_hi))):
                        mm = nc.tensor.matmul(o_ps[:, 0, a0 * P:a1 * P], vt[:, t, hh, :], pt[:, t, a0 * P:a1 * P],
                                              start=(hh == 0 and n == 0 and m == 0),
                                              stop=(hh == 1 and n == 5 and m == 2))
                mm.then_inc(npv_done, 1)

            LATENT = PARTS[:1]

            def open_at(i):
                _, _, before, after = A.next_at(i)
                pe.wait_ge(acc_taken[i], before)
                opened[0] = (i, after)
                return acc[i]

            def part(job, n0, n1, ready=None):
                tile, w, parts, done = job
                for n in range(n0, n1):
                    if ready is not None:
                        ready(n)
                    for m, (wt, mv) in enumerate(((w[0], h_hi), (w[0], h_lo), (w[1], h_hi))):
                        for c0, cn, _ in parts:
                            mm = nc.tensor.matmul(tile[:, c0:c0 + cn], wt[:, n * P:(n + 1) * P], mv[:, n, c0:c0 + cn],
                                                  start=(n == 0 and m == 0), stop=(n == KC - 1 and m == 2))
                if n1 == KC:
                    mm.then_inc(done, 1)

            def values_or_keys():
                w = next_chunk()
                return open_at(1), w, PARTS, acc_full

            def queries():
                if q_left.began():
                    pe.wait_ge(q_taken, q_left.now())
                q_left.up()
                return o_ps[:, 3, :], next_chunk(), LATENT, q_full

            def turn_pair_values():
                tile = open_at(0)
                for t in range(TT):
                    mm = nc.tensor.transpose(tile[:, t * P:(t + 1) * P], S[2][:, t * P:(t + 1) * P], ident)
                mm.then_inc(acc_full, 1)

            def pair(following):
                pe.wait_ge(acc_taken[1], A.taken[1].now())
                pe.wait_ge(q_taken, q_left.now())
                block_scores(0)
                block_scores(1)
                if following:
                    v = values_or_keys()
                    part(v, 0, 4)
                for i in range(8):
                    if i + 2 < 8:
                        block_scores(i + 2)
                    if i == 4:
                        if following:
                            part(k, 3, 5)
                        pair_values(0)
                    turn_probs(i)
                    if following:
                        if i < 2:
                            part(v, 4 + 2 * i, 6 + 2 * i)
                        elif i == 2:
                            k = values_or_keys()
                            part(k, 0, 2)
                        elif i == 3:
                            part(k, 2, 3)
                        elif i == 5:
                            part(k, 5, 6)
                        elif i == 6:
                            part(k, 6, 8)
                            q = queries()
                            part(q, 0, 4)
                        elif i == 7:
                            part(q, 4, 8)
                pair_values(1)
                s_left.up(8)
                pairs_done.up()
                if following:
                    turn_pair_values()

            pe.wait_ge(cond_done, 1)
            start_ada()
            head_front(0, True)
            head_attention()
            steps = [(chunk, 16), (squares_added, VC), (p_split, 8), (o_left, 2), (gates_split, VC)]
            with turns(pe, RH - 1, A.steps(HEAD_TILES + 8) + B.steps(HEAD_SIDE, 1) + steps):
                head_front(None, False)
                head_attention()
            out_projection()
            ones_tile(KC, PARTS)
            ffn(PARTS)
            ones_tile(KC, PARTS)
            ready = h_ready(h_split.now())
            part(values_or_keys(), 0, KC, ready)
            part(values_or_keys(), 0, KC)
            part(queries(), 0, KC)
            pe.wait_ge(set_up, 10)
            turn_pair_values()
            pair(True)
            steps = [(chunk, 6), (s_left, 16), (probs_ready, 16), (pairs_done, 2), (q_left, 2)]
            with turns(pe, (NP - 2) // 2, A.steps_at(18, 4) + steps):
                for _ in range(2):
                    pair(True)
            pair(False)
            h_split.up(KC)
            pe.wait_ge(no_taken, NP + 1)
            with turns(pe, 4, A.steps(2) + [(chunk, 2)]):
                for _ in range(2):
                    project(no_hi, no_lo, LATENT)
            ones_tile(KC, LATENT)
            ffn(LATENT)
            ones_tile(KC, LATENT)

        @block.scalar
        def _(act):
            A, B = AccLine(), AccLine()
            raws, slot = [Tally(), Tally()], [0]
            squares_added, normed, dists, ropes, p_split, value_steps, o_left = (Tally() for _ in range(7))
            gated_chunks, gates_split, convs, products, decays = Tally(), Tally(), Tally(), Tally(), Tally()

            def split():
                i = slot[0]
                slot[0] = 1 - i
                act.wait_ge(raw_in[i], raws[i].up(16))
                nc.scalar.activation(w_hi[i][:, :], raw[i][:, :], ACT.Copy).then_inc(hi_split, 1)

            def wait_full():
                i, full, _, after = A.next()
                act.wait_ge(acc_full, full)
                return i, acc[i]

            def wait_after():
                i, full, _, after = A.next()
                act.wait_ge(acc_full, full)
                return i, after

            def wait_side(got):
                i, full, _, _ = got
                act.wait_ge(side_full, full)
                return i, side[i]

            def squares(src, n, width):
                for k in range(n):
                    if k >= 2:
                        act.wait_ge(sq_added, squares_added.now() + k - 1)
                    nc.scalar.activation(S[k % 2][:, 0:width], src[:, k, 0:width], ACT.Square).then_inc(sq_done, 1)
                squares_added.up(n)

            def root(n, width, on_side=False):
                i, tile = wait_side(B.next_at(0)) if on_side else wait_full()
                nc.scalar.activation(ss[:, 0:width], tile[:, 0:width], ACT.Sqrt, bias=EPS, scale=1.0 / n)\
                  .then_inc((side_taken if on_side else acc_taken)[i], 1)

            def x_final():
                act.wait_ge(acc_taken[0], A.taken[0].now())
                act.wait_ge(acc_taken[1], A.taken[1].now())

            def final_square(i, after, m0, j, width):
                act.wait_ge(acc_taken[i], after)
                act.wait_ge(sq_added, squares_added.up() - 2)
                xm = x[:, bass.ds(m0 + j, 1), 0:width].rearrange("p a t -> p (a t)")
                nc.scalar.activation(S[j % 2][:, 0:width], xm, ACT.Square)\
                  .then_inc(sq_done, 1)

            def norm(layer, shift, parts, rooted=False):
                width = TOK if len(parts) > 1 else LAT
                if not rooted:
                    root(D, width)
                for k in range(KC):
                    act.wait_ge(norm_t, normed.up())
                    for c0, cn, c in parts:
                        ins = nc.scalar.activation(h_hi[:, k, c0:c0 + cn], S[2 + k % 2][:, c0:c0 + cn], ACT.Identity,
                                                   bias=mod[:, layer, shift + k, c:c + 1])
                    ins.then_inc(h_hi_done, 1)

            def take_value(vc):
                i, tile = wait_full()
                nc.scalar.activation(vo[:, vc, :], tile[:, 0:TOK], ACT.Copy).then_inc(acc_taken[i], 1)
                split()

            def value_hi(vc):
                i, tile = wait_side(B.next())
                out_v = vg_hi[:, :].rearrange("p (t v) -> p t v", v=RV)[:, :, vc * P:(vc + 1) * P]
                nc.scalar.activation(out_v, tile[:, 0:TOK].rearrange("p (t v) -> p t v", v=P), ACT.Copy)\
                  .then_inc(v_hi_done, 1)

            def key_hi(j):
                i, tile = wait_full()
                nc.scalar.activation(qk_hi[:, j, LAT:TOK], tile[:, LAT:TOK], ACT.Copy).then_inc(qk_hi_done, 1)
                split()
                act.wait_ge(rope_done, ropes.up())
                nc.scalar.activation(qk_hi[:, j, 0:LAT], S[2][:, 0:LAT], ACT.Copy).then_inc(qk_hi_done, 1)

            def head_front(first):
                if not first:
                    act.wait_ge(gate_lo, gates_split.now())
                take_value(0)
                act.wait_ge(dist_ready, dists.up())
                nc.scalar.activation(near[:, :], S[0][:, :], ACT.Exp, scale=head_logs[:, 0:1]).then_inc(decay_exp, 1)
                nc.scalar.activation(S[1][:, :], S[1][:, :], ACT.Exp, scale=head_logs[:, 1:2]).then_inc(decay_exp, 1)
                nc.scalar.activation(far[:, :], dist[:, 0:640], ACT.Exp, scale=head_logs[:, 0:1], bias=head_logs[:, 2:3])\
                  .then_inc(decay_exp, 1)
                act.wait_ge(decay_exp, decays.up())
                decays.up(3)
                nc.scalar.activation(S[0][:, 0:640], dist[:, 0:640], ACT.Exp, scale=head_logs[:, 3:4], bias=head_logs[:, 4:5])\
                  .then_inc(decay_exp, 1)
                take_value(1)
                if not first:
                    for _ in range(OUT_SLOTS):
                        wait_full()
                        wait_full()
                        split()
                value_hi(0)
                take_value(2)
                value_hi(1)
                take_value(3)
                value_hi(2)
                key_hi(0)
                value_hi(3)
                for j in range(1, 4):
                    key_hi(j)

            def gate(g, i, tile):
                nc.scalar.activation(S[2 + g % 2][:, 0:TOK], tile[:, 0:TOK], ACT.Silu).then_inc(acc_taken[i], 1)
                split()

            def head_attention():
                v0 = value_steps.now()
                queries_taken = A.taken[1 - A.turn].now()
                i, tile = wait_full()
                act.wait_ge(acc_taken[1 - i], queries_taken)
                gate(0, i, tile)
                for i in range(8):
                    qn = SCORES[i][2]
                    t, _, _, after = A.next()
                    act.wait_ge(acc_taken[t], after)
                    if i == 2:
                        act.wait_ge(pv_done, v0 + 1)
                        nc.scalar.activation(vo[:, :, LAT:TOK], o_ps[:, :, 0:CTX], ACT.Copy).then_inc(o_taken, 1)
                    elif i > 3:
                        act.wait_ge(pv_done, v0 + (i - 2))
                    nc.scalar.activation(p_hi[i % 2][:, 0:qn], S[i % 2][:, 0:qn], ACT.Copy).then_inc(p_hi_done, 1)
                act.wait_ge(pv_done, value_steps.up(7))
                nc.scalar.activation(vo[:, :, 0:LAT], o_ps[:, :, :], ACT.Copy).then_inc(o_taken, 1)
                act.wait_ge(p_lo_done, p_split.up(8))
                act.wait_ge(o_taken, o_left.up(2))
                squares(vo, VC, TOK)
                gate(1, *wait_full())
                root(RV, TOK, on_side=True)

                def gated_hi(g):
                    act.wait_ge(gate_mul, gated_chunks.up())
                    nc.scalar.activation(vg_hi[:, g * TOK:(g + 1) * TOK], vo[:, g, :], ACT.Copy).then_inc(gate_hi, 1)

                gated_hi(0)
                for g in range(2, 4):
                    i, tile = wait_full()
                    if g == 3:
                        gated_hi(1)
                    gate(g, i, tile)
                gated_hi(2)
                gated_hi(3)
                gates_split.up(4)

            def ffn(layer, parts, ends):
                width = parts[-1][0] + parts[-1][1]
                for n, size in enumerate(GROUPS):
                    with turns(act, size, A.steps(2) + [(raws[0], 16), (raws[1], 16), (convs, 2), (products, 1)]) as f:
                        nc.scalar.activation(nothing[:, :], silu_c[:, 0, 0:1], ACT.Silu)
                        for j in range(2):
                            i, tile = wait_full()
                            split()
                            if j == 0:
                                act.wait_ge(conv_done, convs.now() + (layer + 1))
                            for c0, cn, c in parts:
                                ins = nc.scalar.activation(u[j][:, c0 + c + 1:c0 + c + 1 + cn], tile[:, c0:c0 + cn], ACT.Copy)
                            ins.then_inc(acc_taken[i], 1)
                        act.wait_ge(conv_done, convs.now() + (layer + 2))
                        w = width + (len(parts) > 1)
                        nc.scalar.activation(S[2][:, 0:w], S[0][:, 0:w], ACT.Silu).then_inc(silu_done, 1)
                        convs.up(2)
                        act.wait_ge(act_mul, products.up())
                        nc.scalar.activation(act_hi[:, bass.ds(f, 1), 0:width].rearrange("p a t -> p (a t)"),
                                             S[3][:, 0:width], ACT.Copy).then_inc(act_hi_done, 1)
                    last = n == len(GROUPS) - 1
                    pairs = 3 if ends and last else 4
                    with turns(act, pairs, A.steps(2) + [(raws[0], 16), (raws[1], 16), (squares_added, 2 * last)]) as i:
                        for m in range(2):
                            t, after = wait_after()
                            split()
                            if last:
                                final_square(t, after, 2 * i, m, width)
                    if pairs == 3:
                        for m in range(2):
                            t, after = wait_after()
                            final_square(t, after, 6, m, width)

            act.wait_ge(const_in, 16)
            nc.scalar.activation(silu_c[:, :, :], cond, ACT.Silu).then_inc(cond_done, 1)
            nc.scalar.activation(logs[:, :, 0:2], cols["dlog"].rearrange("p (h c) -> p h c", c=2), ACT.Exp)\
              .then_inc(cond_done, 1)
            act.wait_ge(rows_in, 32)
            nc.scalar.activation(silu_rows[:, :, :], silu_rows[:, :, :], ACT.Silu).then_inc(cond_done, 1)
            A.next(counted=False)
            act.wait_ge(x_loaded, 16)
            squares(x, KC, TOK)
            root(D, TOK)
            for _ in range(2):
                split()
            norm(0, 0, PARTS, rooted=True)
            head_front(True)
            head_attention()
            steps = [(raws[0], 128), (raws[1], 128), (squares_added, VC), (dists, 1), (decays, 4), (ropes, 4), (p_split, 8)]
            steps += [(value_steps, 7), (o_left, 2), (gated_chunks, 4), (gates_split, 4)]
            with turns(act, RH - 1, A.steps(HEAD_TILES + 8) + B.steps(HEAD_SIDE, 1) + steps):
                head_front(False)
                head_attention()
            for c in range(OUT_SLOTS):
                for m in range(2):
                    t, after = wait_after()
                    if m:
                        split()
                    final_square(t, after, 2 * c, m, TOK)
            x_final()
            norm(0, 24, PARTS)
            ffn(0, PARTS, False)
            x_final()
            norm(1, 0, PARTS)
            maxima, values_done, q_tiles = Tally(), Tally(), Tally()

            def wait_at(i):
                _, full, _, after = A.next_at(i)
                act.wait_ge(acc_full, full)
                return i, acc[i]

            def exps(i):
                hh, a = divmod(i, QB)
                wn = WIN[a][1] * ROWS
                c0 = WIN[a][0] * ROWS - TILES[a][0] * P
                c1 = TILES[a][1] * P
                act.wait_ge(max_done, maxima.up())
                nc.scalar.activation(prob[a][:, c0:c0 + wn], S[i % 2][:, 0:wn], ACT.Exp, bias=top[:, i % 2, 1:2],
                                     accum_out=top[:, i % 2, 2:3])
                nc.scalar.activation(prob[a][:, c1:c1 + CTX], S[i % 2][:, wn:wn + CTX], ACT.Exp, bias=top[:, i % 2, 1:2],
                                     accum_out=top[:, i % 2, 3:4]).then_inc(exp_done, 1)

            def probs_hi(i):
                a = i % QB
                t, tile = wait_at(0)
                if i == 4:
                    act.wait_ge(npv_done, values_done.now() + 1)
                t0, tn = TILES[a]
                nc.scalar.activation(pt_hi[:, t0:t0 + tn, a * P:(a + 1) * P],
                                     tile[:, 0:tn * P].rearrange("p (t q) -> p t q", q=P), ACT.Copy)
                nc.scalar.activation(pt_hi[:, 4:6, a * P:(a + 1) * P],
                                     tile[:, tn * P:(tn + 2) * P].rearrange("p (t q) -> p t q", q=P), ACT.Copy)\
                  .then_inc(pt_hi_done, 1)

            def take_values():
                _, tile = wait_at(1)
                nc.scalar.activation(S[2][:, 0:TOK], tile[:, 0:TOK], ACT.Copy).then_inc(acc_taken[1], 1)
                split()

            def take_keys():
                _, tile = wait_at(1)
                for hh in range(2):
                    for half in range(2):
                        nc.scalar.activation(nk_hi[half * ND:(half + 1) * ND, hh, :], tile[hh * ND:(hh + 1) * ND, 0:TOK],
                                             ACT.Copy).then_inc(n_hi_done, 1)
                split()

            def take_queries():
                act.wait_ge(q_full, q_tiles.up())
                for hh in range(2):
                    nc.scalar.activation(nq[0:ND, hh, :], o_ps[hh * ND:(hh + 1) * ND, 3, :], ACT.Copy, scale=ND ** -0.5)\
                      .then_inc(n_hi_done, 1)
                split()

            def take_turned_values():
                _, tile = wait_at(0)
                for hh in range(2):
                    own = slice(hh * ND, (hh + 1) * ND)
                    nc.scalar.activation(nv_hi[:, :, hh, own], tile[:, 0:TOK].rearrange("p (t v) -> p t v", v=P)[:, :, own],
                                         ACT.Copy).then_inc(n_hi_done, 1)

            def pair(c, following):
                exps(0)
                exps(1)
                for i in range(8):
                    probs_hi(i)
                    if i + 2 < 8:
                        exps(i + 2)
                    if following and i == 1:
                        take_values()
                    if following and i == 6:
                        take_keys()
                if following:
                    take_queries()
                act.wait_ge(npv_done, values_done.up(2))
                nc.scalar.activation(no_hi[:, bass.ds(c, 1), :].rearrange("p a t -> p (a t)"), o_ps[:, 0, :], ACT.Copy)\
                  .then_inc(n_hi_done, 1)
                if following:
                    take_turned_values()

            take_values()
            take_keys()
            take_queries()
            act.wait_ge(set_up, 10)
            take_turned_values()
            act.wait_ge(parked, 16)
            pair(0, True)
            steps = [(raws[0], 48), (raws[1], 48), (maxima, 16), (values_done, 4), (q_tiles, 2)]
            with turns(act, (NP - 2) // 2, A.steps_at(18, 4) + steps) as i:
                for j in range(2):
                    pair(2 * i + (1 + j), True)
            pair(NP - 1, False)
            with turns(act, 4, A.steps(2) + [(raws[0], 16), (raws[1], 16), (squares_added, 2)]) as i:
                for m in range(2):
                    t, after = wait_after()
                    split()
                    final_square(t, after, 2 * i, m, LAT)
            x_final()
            norm(1, 24, PARTS[:1])
            ffn(1, PARTS[:1], True)
            root(D, LAT)

        @block.vector
        def _(dve):
            A, B = AccLine(), AccLine()
            hi_splits, slot = Tally(), [0]
            h_split, ada_loads, own_steps, squares_made, h_hi_made, ada_made = (Tally() for _ in range(6))
            decays, v_hi_made, qk_hi_made, p_hi_made, gate_hi_made, act_hi_made = (Tally() for _ in range(6))
            silus, normed = Tally(), Tally()

            def step(ins):
                ins.then_inc(vec_step, 1)
                dve.wait_ge(vec_step, own_steps.up())

            def split():
                i = slot[0]
                slot[0] = 1 - i
                dve.wait_ge(hi_split, hi_splits.up())
                nc.vector.tensor_tensor(w_lo[i][:, :], raw[i][:, :], w_hi[i][:, :].bitcast(F32), ALU.subtract)\
                  .then_inc(lo_split, 1)

            def wait_full():
                i, full, _, after = A.next()
                dve.wait_ge(acc_full, full)
                return i, acc[i]

            def own_done():
                dve.wait_ge(acc_taken[0], A.taken[0].now())
                dve.wait_ge(acc_taken[1], A.taken[1].now())

            def add_squares(n, width):
                for k in range(n):
                    dve.wait_ge(sq_done, squares_made.up())
                    if k == 0:
                        ins = nc.vector.tensor_copy(ss[:, 0:width], S[0][:, 0:width])
                    else:
                        dve.wait_ge(sq_added, squares_made.now() - 1)
                        ins = nc.vector.tensor_tensor(ss[:, 0:width], ss[:, 0:width], S[k % 2][:, 0:width], ALU.add)
                    ins.then_inc(sq_added, 1)

            def add_square(j, width):
                dve.wait_ge(sq_done, squares_made.up())
                dve.wait_ge(sq_added, squares_made.now() - 1)
                nc.vector.tensor_tensor(ss[:, 0:width], ss[:, 0:width], S[j][:, 0:width], ALU.add).then_inc(sq_added, 1)

            def one_over(width, on_side=False):
                i, _, _, after = B.next_at(0) if on_side else A.next()
                dve.wait_ge((side_taken if on_side else acc_taken)[i], after)
                step(nc.vector.reciprocal(ss[:, 0:width], ss[:, 0:width]))

            def take_start():
                i, _, _, after = A.next(counted=False)
                for j in range(KC):
                    at = 2 + j // 4
                    if j == 4:
                        add_squares(KC, TOK)
                        one_over(TOK)
                    dve.wait_ge(ada_start_in[at], 16)
                    place = ada_start[at][:, j % 4, :]
                    step(nc.vector.tensor_tensor_reduce(S[3][:, :], place, silu_rows[:, 1, :], 1.0, 0.0, ALU.mult,
                                                        ALU.add, mod_new[:, j, 1:2]))
                    step(nc.vector.tensor_tensor_reduce(place, place, silu_rows[:, 0, :], 1.0, 0.0, ALU.mult, ALU.add,
                                                        mod_new[:, j, 0:1]))
                products = [(KC, mod_new[:, :, :])]
                products.append((0, acc[i][:, 0:2 * KC].rearrange("p (j c) -> p j c", c=2)))
                for at, made in products:
                    if at == 0:
                        dve.wait_ge(ada_started, 1)
                    ins = nc.vector.tensor_tensor(mod[:, 0, at:at + KC, :], made,
                                                  ada_b[:, 0, at:at + KC].rearrange("p (j c) -> p j c", c=1)
                                                  .to_broadcast([P, KC, 2]), ALU.add)
                    if at:
                        step(ins)
                ins.then_inc(acc_taken[i], 1)

            def ada_step(j, waste, conds=2):
                dve.wait_ge(ada_in, ada_loads.up(16))
                if conds == 2:
                    step(nc.vector.tensor_tensor_reduce(waste[:, 0:D], ada_raw[:, :], silu_rows[:, 1, :], 1.0, 0.0, ALU.mult,
                                                        ALU.add, mod_new[:, j, 1:2]))
                nc.vector.tensor_tensor_reduce(ada_raw[:, :], ada_raw[:, :], silu_rows[:, 0, :], 1.0, 0.0, ALU.mult, ALU.add,
                                               mod_new[:, j, 0:1]).then_inc(ada_used, 1)
                ada_made.up()

            def take_ada(layer, j, n, conds=2):
                dve.wait_ge(ada_used, ada_made.now())
                step(nc.vector.tensor_tensor(mod[:, layer, bass.ds(j, n), 0:conds], mod_new[:, 0:n, 0:conds],
                                             ada_b[:, layer, bass.ds(j, n)].rearrange("p (j c) -> p j c", c=1)
                                             .to_broadcast([P, n, conds]), ALU.add))

            def norm(layer, which, shift, parts, by_column, inverted=False):
                width = TOK if len(parts) > 1 else LAT
                n = len(parts)
                own_done()
                step(nc.vector.scalar_tensor_tensor(
                    norm_a[:, :, 0:n], mod[:, layer, shift + KC:shift + 2 * KC, 0:n], 1.0,
                    norm_w[:, which, :].rearrange("p (k c) -> p k c", c=1).to_broadcast([P, KC, n]), ALU.add, ALU.mult))
                if not inverted:
                    one_over(width)

                def scaled(k):
                    for c0, cn, c in parts:
                        o, a, b = (z[:, c0:c0 + cn] for z in (S[2 + k % 2], x[:, k, :], ss))
                        if by_column and c == 0:
                            o = o.rearrange("p (c r) -> p r c", r=ROWS)
                            a, b = (z.rearrange("p (r c) -> p r c", c=COLS) for z in (a, b))
                        ins = nc.vector.scalar_tensor_tensor(o, a, norm_a[:, k, c:c + 1], b, ALU.mult, ALU.mult)
                    ins.then_inc(norm_t, 1)

                scaled(0)
                scaled(1)
                for k in range(KC):
                    dve.wait_ge(norm_t, normed.up())
                    dve.wait_ge(h_hi_done, h_hi_made.up())
                    for c0, cn, c in parts:
                        ins = nc.vector.scalar_tensor_tensor(h_lo[:, k, c0:c0 + cn], S[2 + k % 2][:, c0:c0 + cn],
                                                             mod[:, layer, shift + k, c:c + 1],
                                                             h_hi[:, k, c0:c0 + cn].bitcast(F32), ALU.add, ALU.subtract)
                    ins.then_inc(h_lo_done, 1)
                    if k + 2 < KC:
                        dve.wait_ge(h_lo_done, h_split.up())
                        scaled(k + 2)
                h_split.up(2)

            def add_gated(m, layer, gate, parts):
                i, tile = wait_full()
                for c0, cn, c in parts:
                    xv = x[:, bass.ds(m, 1), c0:c0 + cn].rearrange("p a t -> p (a t)")
                    ins = nc.vector.scalar_tensor_tensor(
                        xv, tile[:, c0:c0 + cn],
                        mod[:, layer, bass.ds(gate + m, 1), c:c + 1].rearrange("p a c -> p (a c)"), xv, ALU.mult, ALU.add)
                ins.then_inc(acc_taken[i], 1)

            def out_projection(with_ada, final=False):
                if final:
                    step(nc.vector.memset(ss[:, :], 0.0))
                own_done()
                for m in range(KC):
                    add_gated(m, 0, 16, PARTS)
                    if m % 2:
                        split()
                    if final:
                        add_square(m % 2, TOK)
                    if m % 2:
                        if m < 2 * with_ada:
                            ada_step(m // 2, S[3])

            def value_lo(vc):
                i, full, _, _ = B.next()
                dve.wait_ge(side_full, full)
                tile = side[i]
                dve.wait_ge(v_hi_done, v_hi_made.up())
                hi, lo = (z[:, :].rearrange("p (t v) -> p t v", v=RV)[:, :, vc * P:(vc + 1) * P] for z in (vg_hi, vg_lo))
                nc.vector.tensor_tensor(lo, tile[:, 0:TOK].rearrange("p (t v) -> p t v", v=P), hi.bitcast(F32),
                                        ALU.subtract).then_inc(side_taken[i], 1)

            def rotated(j):
                i, tile = wait_full()
                if j % 2 == 0:
                    table = lambda z, p0, p1: z[p0:p1, :].rearrange("p (r c) -> p r c", c=1).to_broadcast([p1 - p0, ROWS, COLS])
                    cos, sin = cols["cos_r"], cols["sin_r"]
                else:
                    table = lambda z, p0, p1: z[p0:p1, :].rearrange("p (r c) -> p r c", r=1).to_broadcast([p1 - p0, ROWS, COLS])
                    cos, sin = cols["cos_c"], cols["sin_c"]
                grid = lambda z, p0, p1: z[p0:p1, 0:LAT].rearrange("p (r c) -> p r c", c=COLS)
                nc.vector.tensor_tensor(grid(S[0], 0, P), grid(tile, 0, P), table(cos, 0, P), ALU.mult)
                nc.vector.tensor_tensor(grid(S[1], 0, 64), grid(tile, 64, P), table(sin, 64, P), ALU.mult)
                nc.vector.tensor_tensor(grid(S[1], 64, P), grid(tile, 0, 64), table(sin, 0, 64), ALU.mult).then_inc(vec_step, 1)
                split()
                dve.wait_ge(vec_step, own_steps.up())
                nc.vector.tensor_tensor(S[2][:, 0:LAT], S[0][:, 0:LAT], S[1][:, 0:LAT], ALU.add).then_inc(rope_done, 1)
                dve.wait_ge(qk_hi_done, qk_hi_made.up(2))
                nc.vector.tensor_tensor(qk_lo[:, j, 0:LAT], S[2][:, 0:LAT], qk_hi[:, j, 0:LAT].bitcast(F32), ALU.subtract)
                nc.vector.tensor_tensor(qk_lo[:, j, LAT:TOK], tile[:, LAT:TOK], qk_hi[:, j, LAT:TOK].bitcast(F32),
                                        ALU.subtract).then_inc(acc_taken[i], 1)

            def only_split():
                wait_full()
                split()

            def head_front(hd, first):
                only_split()
                if first:
                    ada_step(0, S[3])
                nc.vector.tensor_copy(head_logs[:, :], logs[:, bass.ds(hd, 1), :].rearrange("p a c -> p (a c)"))
                nc.vector.tensor_scalar(S[0][:, :], dist[:, :], 0.0, None, ALU.max)
                nc.vector.tensor_scalar(S[1][:, :], dist[:, :], -1.0, 0.0, ALU.mult, ALU.max).then_inc(dist_ready, 1)
                only_split()
                dve.wait_ge(decay_exp, decays.up(4))
                nc.vector.tensor_tensor(near[:, :], near[:, :], S[1][:, :], ALU.mult)
                step(nc.vector.tensor_tensor(far[:, :], far[:, :], S[0][:, 0:640], ALU.add))
                if first:
                    ada_step(1, S[3])
                    ada_step(2, S[3])
                else:
                    out_projection(3)
                value_lo(0)
                only_split()
                ada_step(3, S[3])
                value_lo(1)
                only_split()
                ada_step(4, S[3])
                value_lo(2)
                rotated(0)
                ada_step(5, S[3])
                value_lo(3)
                for j in range(1, 4):
                    rotated(j)
                    if j < 3:
                        ada_step(5 + j, S[3])
                take_ada(0, hd * 8 + 16, 8)
                only_split()

            def head_attention():
                for i in range(8):
                    _, _, qn, table, c0, _ = SCORES[i]
                    t, tile = wait_full()
                    nc.vector.scalar_tensor_tensor(S[i % 2][:, 0:qn], tile[:, 0:qn], RQK ** -0.5, table[:, c0:c0 + qn],
                                                   ALU.mult, ALU.mult).then_inc(acc_taken[t], 1)
                    dve.wait_ge(p_hi_done, p_hi_made.up())
                    nc.vector.tensor_tensor(p_lo[i % 2][:, 0:qn], S[i % 2][:, 0:qn], p_hi[i % 2][:, 0:qn].bitcast(F32),
                                            ALU.subtract).then_inc(p_lo_done, 1)
                add_squares(VC, TOK)

                def gated(g):
                    step(nc.vector.tensor_tensor(vo[:, g, :], vo[:, g, :], ss[:, :], ALU.mult))
                    nc.vector.tensor_tensor(vo[:, g, :], vo[:, g, :], S[2 + g % 2][:, 0:TOK], ALU.mult).then_inc(gate_mul, 1)

                def gated_lo(g):
                    dve.wait_ge(gate_hi, gate_hi_made.up())
                    nc.vector.tensor_tensor(vg_lo[:, g * TOK:(g + 1) * TOK], vo[:, g, :],
                                            vg_hi[:, g * TOK:(g + 1) * TOK].bitcast(F32), ALU.subtract).then_inc(gate_lo, 1)

                only_split()
                one_over(TOK, on_side=True)
                own_done()
                gated(0)
                gated(1)
                gated_lo(0)
                for g in range(2, 4):
                    i, _, _, after = A.next()
                    dve.wait_ge(acc_full, A.full.now())
                    split()
                    dve.wait_ge(acc_taken[i], after)
                    if g == 2:
                        gated(2)
                        gated_lo(1)
                    else:
                        gated(3)
                gated_lo(2)
                gated_lo(3)

            def ffn(layer, parts, with_ada, ends):
                nj = 0
                w_all = parts[-1][0] + parts[-1][1]
                width = TOK + 1 if len(parts) > 1 else LAT
                f0 = 0
                for n, size in enumerate(GROUPS):
                    conds = 2 if n == 0 else 1
                    ups = UP_ADA[n] if with_ada else 0
                    steps = [(hi_splits, 2), (own_steps, 5 + ups * conds), (silus, 1), (act_hi_made, 1)]
                    steps += [(ada_loads, 16 * ups), (ada_made, ups)]
                    with turns(dve, size, A.steps(2) + steps) as f:
                        step(nc.vector.tensor_copy(taps[:, :], conv[:, layer, bass.ds(f + f0, 1), :].rearrange("p a c -> p (a c)")))
                        for j in range(2):
                            i, _, _, after = A.next()
                            dve.wait_ge(acc_full, A.full.now())
                            split()
                            dve.wait_ge(acc_taken[i], after)
                            tap = lambda t: taps[:, 4 * j + t:4 * j + t + 1]
                            step(nc.vector.tensor_scalar(S[j][:, 0:width], u[j][:, 0:width], tap(0), tap(3), ALU.mult, ALU.add))
                            step(nc.vector.scalar_tensor_tensor(S[j][:, 0:width], u[j][:, 1:1 + width], tap(1), S[j][:, 0:width],
                                                                ALU.mult, ALU.add))
                            nc.vector.scalar_tensor_tensor(S[j][:, 0:width], u[j][:, 2:2 + width], tap(2), S[j][:, 0:width],
                                                           ALU.mult, ALU.add).then_inc(conv_done, 1)
                            if ups and j == 0:
                                ada_step(0, waste, conds)
                        dve.wait_ge(silu_done, silus.up())
                        dve.wait_ge(conv_done, silus.now() * 2 + (layer + 1))
                        for c0, cn, c in parts:
                            ins = nc.vector.tensor_tensor(S[3][:, c0:c0 + cn], S[2][:, c0 + c:c0 + c + cn],
                                                          S[1][:, c0 + c:c0 + c + cn], ALU.mult)
                        ins.then_inc(act_mul, 1)
                        dve.wait_ge(act_hi_done, act_hi_made.up())
                        w = parts[-1][0] + parts[-1][1]
                        hi, lo = (z[:, bass.ds(f, 1), 0:w].rearrange("p a t -> p (a t)") for z in (act_hi, act_lo))
                        nc.vector.tensor_tensor(lo, S[3][:, 0:w], hi.bitcast(F32), ALU.subtract).then_inc(act_lo_done, 1)
                        if ups:
                            take_ada(1, f + nj, 1, conds)
                    f0 += size
                    nj += ups * size
                    own_done()
                    pairs = 3 if ends and n == 2 else 4
                    loads = DOWN_ADA[n] if with_ada else 0
                    last = n == len(GROUPS) - 1
                    if last:
                        step(nc.vector.memset(ss[:, :], 0.0))
                    steps = [(hi_splits, 2), (ada_loads, 16 * loads), (ada_made, loads), (squares_made, 2 * last)]
                    steps += [(own_steps, 1 + loads * (conds - 1))] if loads else []
                    with turns(dve, pairs, A.steps(2) + steps) as i:
                        for m in range(2):
                            add_gated(2 * i + m, layer, 40, parts)
                            split()
                            if last:
                                add_square(m, w_all)
                            if loads:
                                ada_step(m, waste, conds)
                        if loads == 3:
                            ada_step(2, waste, conds)
                        if loads:
                            take_ada(1, i * loads + nj, loads, conds)
                    nj += 4 * loads
                    if pairs == 3:
                        for m in range(2):
                            add_gated(6 + m, layer, 40, parts)
                            add_square(m, w_all)

            def pads():
                for j in range(2):
                    for c in (0, LAT + 1, TOK + 2):
                        ins = nc.vector.memset(u[j][:, c:c + 1], 0.0)
                ins.then_inc(conv_done, 1)

            dve.wait_ge(const_in, 16)
            dve.wait_ge(cond_done, 3)
            step(nc.vector.tensor_scalar(logs[:, :, 0:2], logs[:, :, 0:2], -1.0, None, ALU.mult))
            nc.vector.tensor_scalar(logs[:, :, 2:3], logs[:, :, 0:1], 512.0, None, ALU.mult)
            nc.vector.tensor_scalar(logs[:, :, 3:4], logs[:, :, 1:2], -1.0, None, ALU.mult)
            nc.vector.tensor_scalar(logs[:, :, 4:5], logs[:, :, 1:2], 256.0, None, ALU.mult)
            step(nc.vector.memset(logs[:, :, 5:8], 0.0))
            take_start()
            dve.wait_ge(x_loaded, 16)
            for _ in range(2):
                split()
            dve.wait_ge(set_up, 2)
            norm(0, 0, 0, PARTS, False, inverted=True)
            head_front(0, True)
            head_attention()
            steps = [(ada_loads, 128), (hi_splits, 16), (own_steps, 19), (squares_made, VC), (ada_made, 8), (decays, 4)]
            steps += [(v_hi_made, 4), (qk_hi_made, 8), (p_hi_made, 8), (gate_hi_made, 4)]
            with turns(dve, RH - 1, A.steps(HEAD_TILES + 8) + B.steps(HEAD_SIDE, 1) + steps) as hd:
                head_front(hd + 1, False)
                head_attention()
            out_projection(0, final=True)
            pads()
            norm(0, 2, 24, PARTS, False)
            ffn(0, PARTS, True, False)
            norm(1, 1, 0, PARTS, True)
            n_hi_made, score_tiles, exps_made, pt_hi_made, biases_made, q_tiles = (Tally() for _ in range(6))

            def wait_at(i):
                _, full, _, _ = A.next_at(i)
                dve.wait_ge(acc_full, full)
                return i, acc[i]

            def maximum(i):
                hh, a = divmod(i, QB)
                n = WIN[a][1] * ROWS + CTX
                dve.wait_ge(s_full, score_tiles.up())
                nc.vector.memset(top[:, i % 2, 5:6], 0.0)
                nc.vector.tensor_tensor_reduce(S[i % 2][:, 0:n], o_ps[:, 1 + i % 2, 0:n], bias[hh][:, MASKS[a], 0:n], 1.0, -3e38,
                                               ALU.add, ALU.max, top[:, i % 2, 0:1]).then_inc(s_taken, 1)
                dve.wait_ge(s_taken, score_tiles.now() + 1)
                nc.vector.tensor_scalar(top[:, i % 2, 1:2], top[:, i % 2, 0:1], -1.0, None, ALU.mult).then_inc(max_done, 1)

            def scale_probs(i):
                dve.wait_ge(exp_done, exps_made.up())
                step(nc.vector.tensor_tensor(top[:, i % 2, 4:5], top[:, i % 2, 2:3], top[:, i % 2, 3:4], ALU.add))
                step(nc.vector.reciprocal(top[:, i % 2, 4:5], top[:, i % 2, 4:5]))
                nc.vector.tensor_scalar(prob[i % QB][:, :], prob[i % QB][:, :], top[:, i % 2, 4:5], None, ALU.mult)\
                  .then_inc(prob_done, 1)

            def probs_lo(i):
                a = i % QB
                t, tile = wait_at(0)
                dve.wait_ge(pt_hi_done, pt_hi_made.up())
                t0, normed = TILES[a]
                for z0, zn, c0 in ((t0, normed, 0), (4, 2, normed * P)):
                    hi, lo = (z[:, z0:z0 + zn, a * P:(a + 1) * P] for z in (pt_hi, pt_lo))
                    ins = nc.vector.tensor_tensor(lo, tile[:, c0:c0 + zn * P].rearrange("p (t q) -> p t q", q=P),
                                                  hi.bitcast(F32), ALU.subtract)
                ins.then_inc(acc_taken[t], 1)

            def take_keys():
                t, tile = wait_at(1)
                for hh in range(2):
                    dve.wait_ge(n_hi_done, n_hi_made.up(2))
                    for half in range(2):
                        own = slice(half * ND, (half + 1) * ND)
                        ins = nc.vector.tensor_tensor(nk_lo[own, hh, :], tile[hh * ND:(hh + 1) * ND, 0:TOK],
                                                      nk_hi[own, hh, :].bitcast(F32), ALU.subtract)
                ins.then_inc(acc_taken[t], 1)

            def take_queries():
                dve.wait_ge(q_full, q_tiles.up())
                for hh in range(2):
                    dve.wait_ge(n_hi_done, n_hi_made.up())
                    ins = nc.vector.scalar_tensor_tensor(nq[ND:P, hh, :], o_ps[hh * ND:(hh + 1) * ND, 3, :], ND ** -0.5,
                                                         nq[0:ND, hh, :].bitcast(F32), ALU.mult, ALU.subtract)
                ins.then_inc(q_taken, 1)
                split()

            def take_turned_values():
                t, tile = wait_at(0)
                dve.wait_ge(n_hi_done, n_hi_made.up(2))
                for hh in range(2):
                    own = slice(hh * ND, (hh + 1) * ND)
                    ins = nc.vector.tensor_tensor(nv_lo[:, :, hh, own], tile[:, 0:TOK].rearrange("p (t v) -> p t v", v=P)[:, :, own],
                                                  nv_hi[:, :, hh, own].bitcast(F32), ALU.subtract)
                ins.then_inc(acc_taken[t], 1)

            def pair(c, following):
                dve.wait_ge(bias_done, biases_made.up(6))
                maximum(0)
                maximum(1)
                scale_probs(0)
                for i in range(8):
                    if i + 2 < 8:
                        maximum(i + 2)
                    if i + 1 < 8:
                        scale_probs(i + 1)
                    probs_lo(i)
                    if following:
                        if i == 1:
                            A.next_at(1)
                        if i == 2:
                            split()
                        if i == 6:
                            take_keys()
                        if i == 7:
                            split()
                if following:
                    take_queries()
                dve.wait_ge(n_hi_done, n_hi_made.up(1))
                hi, lo = (z[:, bass.ds(c, 1), :].rearrange("p a t -> p (a t)") for z in (no_hi, no_lo))
                nc.vector.tensor_tensor(lo, o_ps[:, 0, :], hi.bitcast(F32), ALU.subtract).then_inc(no_taken, 1)
                if following:
                    take_turned_values()

            nc.vector.memset(top[:, 0, 5:6], 0.0).then_inc(s_taken, 1)
            nc.vector.memset(top[:, 1, 5:6], 0.0).then_inc(no_taken, 1)
            wait_at(1)
            split()
            take_keys()
            split()
            take_queries()
            dve.wait_ge(set_up, 10)
            take_turned_values()
            pair(0, True)
            steps = [(hi_splits, 6), (own_steps, 32), (n_hi_made, 18), (score_tiles, 16), (exps_made, 16)]
            steps += [(pt_hi_made, 16), (biases_made, 12), (q_tiles, 2)]
            with turns(dve, (NP - 2) // 2, A.steps_at(18, 4) + steps) as i:
                for j in range(2):
                    pair(2 * i + (1 + j), True)
            pair(NP - 1, False)
            dve.wait_ge(x_back, 16)
            step(nc.vector.memset(ss[:, :], 0.0))
            with turns(dve, 4, A.steps(2) + [(hi_splits, 2), (squares_made, 2)]) as i:
                for m in range(2):
                    t, tile = wait_full()
                    xv = x[:, bass.ds(2 * i + m, 1), 0:LAT].rearrange("p a (r c) -> p c (a r)", c=COLS)
                    nc.vector.scalar_tensor_tensor(
                        xv, tile[:, 0:LAT].rearrange("p (c r) -> p c r", r=ROWS),
                        mod[:, 1, bass.ds(2 * i + (16 + m), 1), 0:1].rearrange("p a c -> p (a c)"), xv,
                        ALU.mult, ALU.add).then_inc(acc_taken[t], 1)
                    split()
                    add_square(m, LAT)
            pads()
            norm(1, 3, 24, PARTS[:1], False)
            ffn(1, PARTS[:1], False, True)
            own_done()
            one_over(LAT)
            for k in range(KC):
                step(nc.vector.tensor_tensor(x[:, k, 0:LAT], x[:, k, 0:LAT], ss[:, 0:LAT], ALU.mult))
                nc.vector.tensor_scalar(x[:, k, 0:LAT], x[:, k, 0:LAT], norm_w[:, 4, k:k + 1], None, ALU.mult)\
                  .then_inc(x_ready, 1)


def tiled(w):
    *lead, k, m = w.shape
    n = len(lead)
    w = w.reshape(*lead, k // P, P, m // P, P)
    return w.transpose(*range(n), n + 2, n + 1, n, n + 3)


def weight_stream(w_in, r_out, w_qkv, n_out, up, down):
    chunks = []
    put = lambda c: chunks.append(np.ascontiguousarray(c).reshape(P, D))
    win = tiled(w_in)
    ro = tiled(r_out.reshape(RH, RV, D))
    qk, v, g = RH * 2, RH * 4, RH * 8

    def put_out(h):
        for s in range(OUT_SLOTS):
            put(ro[h, 2 * s:2 * s + 2].transpose(1, 0, 2, 3))

    def put_ffn(layer):
        u = tiled(up[layer])
        f0 = 0
        for size in GROUPS:
            for f in range(f0, f0 + size):
                put(u[f])
                put(u[FC + f])
            dn = tiled(down[layer][f0 * P:(f0 + size) * P])
            for m in range(KC):
                put(np.pad(dn[m], ((0, 0), (0, 8 - size), (0, 0))))
            f0 += size

    for h in range(RH):
        put(win[2 * qk + 4 * h])
        put(win[2 * qk + 4 * h + 1])
        if h:
            put_out(h - 1)
        put(win[2 * qk + 4 * h + 2])
        put(win[2 * qk + 4 * h + 3])
        for j in range(2):
            put(win[qk + 2 * h + j])
        for j in range(2):
            put(win[2 * h + j])
        for j in range(4):
            put(win[2 * qk + RH * 4 + 4 * h + j])
    put_out(RH - 1)
    put_ffn(0)
    qkv = tiled(w_qkv)
    for c in range(NP):
        for j in (2, 1, 0):
            put(qkv[j * KC + c])
    no = tiled(n_out)
    for m in range(KC):
        put(no[m])
    put_ffn(1)
    assert len(chunks) == CHUNKS
    return np.stack(chunks)


def by_feature(a):
    a = a.reshape(*a.shape[:-1], KC, P)
    return np.moveaxis(a, -1, 0)


def rope_tables():
    q = RQK // 4
    inv = np.float32(10000.0) ** (-np.arange(q, dtype=np.float32) / np.float32(q))
    inv = np.concatenate([inv, inv])[:, None].astype(np.float32)
    sign = np.where(np.arange(P) < q, 1, -1)[:, None].astype(np.float32)
    out = []
    for n in (ROWS, COLS):
        ang = np.arange(n, dtype=np.float32)[None, :] * inv
        out += [np.cos(ang).astype(np.float32), (np.sin(ang) * sign).astype(np.float32)]
    return out


def mask_tables():
    c = np.arange(16)[:, None]
    k = np.arange(32)[None, :]
    out = []
    for first in (0, 16, 48):
        query, key = c + first, k + first - 8
        start = np.clip(query - NKW // 2, 0, COLS - NKW)
        ok = (key >= start) & (key < start + NKW)
        m = np.where(ok, 0.0, -1e30).astype(np.float32)
        out.append(np.broadcast_to(m[:, None, :, None], (16, ROWS, 32, ROWS)).reshape(P, 256))
    return np.ascontiguousarray(np.stack(out, 1))


def relative(rpb):
    padded = np.pad(rpb, ((0, 0), (0, 0), (8, 8)))
    c, r = np.divmod(np.arange(P), ROWS)
    k, kr = np.divmod(np.arange(256), ROWS)
    dr = kr[None, :] - r[:, None] + ROWS - 1
    dc = k[None, :] - c[:, None] + 7 + 8
    return np.ascontiguousarray(padded[:, dr, dc])


def kernel(**inputs):
    import concourse.bacc as bacc
    from concourse.bass_utils import run_bass_kernel_spmd

    a = {k: np.asarray(v) for k, v in inputs.items()}
    tokens = np.concatenate([a["x"][0], a["ctx"][0]])
    x_in = np.ascontiguousarray(by_feature(tokens).transpose(0, 2, 1))
    weights = weight_stream(a["ret_w_in"][0], a["ret_w_out"][0], a["na_w_qkv"][0], a["na_w_out"][0],
                            a["ffn_w_up"], a["ffn_w_down"])
    ada = np.ascontiguousarray(a["ada_w"].transpose(0, 2, 1)).reshape(96, P, D)
    ada_first = np.concatenate([tiled(a["ada_w"][0, :, :D]).reshape(KC, P, D), ada[KC:2 * KC]])
    norm_w = np.stack([a["norm1_w"][0], a["norm1_w"][1], a["norm2_w"][0], a["norm2_w"][1], a["final_norm_w"]])
    taps = np.concatenate([a["ffn_conv_w"], a["ffn_conv_b"][:, None]], 1)
    taps = taps.reshape(2, 4, 2, FC, P).transpose(4, 0, 3, 2, 1)
    cos_r, sin_r, cos_c, sin_c = rope_tables()
    parts = {
        "cond": by_feature(np.stack([a["c"][0], a["c_ctx"]])).transpose(0, 2, 1),
        "norm_w": by_feature(norm_w),
        "ada_b": a["ada_b"].reshape(2, 48, P).transpose(2, 0, 1),
        "dlog": np.broadcast_to(np.stack([a["ret_decay_fwd"][0], a["ret_decay_bwd"][0]], 1)[None], (P, RH, 2)),
        "cos_r": cos_r, "sin_r": sin_r, "cos_c": cos_c, "sin_c": sin_c,
        "conv": taps, "ident": np.eye(P, dtype=np.float32),
    }
    small = np.concatenate([np.ascontiguousarray(parts[n]).reshape(P, -1) for n, _ in SMALL], 1)
    arrays = {"x_in": x_in, "weights": weights, "ada_first": ada_first, "ada": ada[2 * KC:].copy(),
              "cond_rows": np.stack([a["c"][0], a["c_ctx"]]), "small": np.ascontiguousarray(small),
              "bias": relative(a["na_rpb"][0]), "masks": mask_tables()}
    nc = bacc.Bacc("TRN2", target_bir_lowering=False, num_devices=1)
    aps = [nc.dram_tensor(f"in_{n}_dram", v.shape, F32, kind="ExternalInput").ap() for n, v in arrays.items()]
    park = nc.dram_tensor("park_dram", (P, KC, LAT), F32, kind="Internal").ap()
    out = nc.dram_tensor("out_dram", (P, KC, LAT), F32, kind="ExternalOutput").ap()
    backbone(nc, *aps, park, out)
    r = run_bass_kernel_spmd(nc, [{f"in_{n}_dram": v for n, v in arrays.items()}], core_ids=[0])
    y = r.results[0]["out_dram"]
    return np.ascontiguousarray(y.transpose(2, 1, 0)).reshape(1, LAT, D)
```
